# Optimizing a Trainium2 kernel written in Bass

```python
import math
import jax, jax.numpy as jnp
from jax import lax
import numpy as np

D_MODEL = 1024
BATCH = 1
SEQ = 256
DEPTH = 1

HEAD_DIM = 64
N_FOX_HEADS = 8
N_DSA_HEADS = 8
N_IDX_HEADS = 4
IDX_DIM = 64
TOPK_MAX = 256
Q_BLOCK = 128
N_BUCKETS = 32
MAX_DISTANCE = 128
D_FF = 4 * D_MODEL
EPS = 1e-6

FOX_W = N_FOX_HEADS * HEAD_DIM
DSA_W = N_DSA_HEADS * HEAD_DIM
SPLIT_SIZES = [
    FOX_W, FOX_W, FOX_W,
    N_FOX_HEADS,
    DSA_W, DSA_W, DSA_W,
    N_IDX_HEADS * IDX_DIM,
    IDX_DIM,
    N_IDX_HEADS,
    D_MODEL, D_MODEL,
]
D_IN = int(sum(SPLIT_SIZES))
SPLIT_POINTS = [int(v) for v in np.cumsum(SPLIT_SIZES)[:-1]]


def rmsnorm(x, g):
    xf = x.astype(jnp.float32)
    y = xf * lax.rsqrt(jnp.mean(xf * xf, axis=-1, keepdims=True) + EPS)
    return (y * g.astype(jnp.float32)).astype(x.dtype)

def t5_bucket(dist):
    n = jnp.maximum(dist, 0)
    max_exact = N_BUCKETS // 2
    is_small = n < max_exact
    nf = jnp.maximum(n, 1).astype(jnp.float32)
    large = max_exact + (jnp.log(nf / max_exact) / math.log(MAX_DISTANCE / max_exact)
                         * (N_BUCKETS - max_exact)).astype(jnp.int32)
    large = jnp.minimum(large, N_BUCKETS - 1)
    return jnp.where(is_small, n, large)

def forgetting_attention(q, k, v, cum_logf):
    B, S, H, Dh = q.shape
    n_blocks = S // Q_BLOCK
    scale = Dh ** -0.5
    Ft = jnp.transpose(cum_logf, (0, 2, 1))
    key_pos = jnp.arange(S)

    def block(i):
        start = i * Q_BLOCK
        qb = lax.dynamic_slice_in_dim(q, start, Q_BLOCK, axis=1)
        Fb = lax.dynamic_slice_in_dim(Ft, start, Q_BLOCK, axis=2)
        s = jnp.einsum('bqhd,bkhd->bhqk', qb, k).astype(jnp.float32) * scale
        s = s + Fb[..., :, None] - Ft[:, :, None, :]
        q_pos = start + jnp.arange(Q_BLOCK)
        mask = key_pos[None, :] <= q_pos[:, None]
        s = jnp.where(mask[None, None], s, -jnp.inf)
        p = jax.nn.softmax(s, axis=-1).astype(v.dtype)
        return jnp.einsum('bhqk,bkhd->bqhd', p, v)

    out = lax.map(block, jnp.arange(n_blocks))
    return jnp.transpose(out, (1, 0, 2, 3, 4)).reshape(B, S, H, Dh)

def indexer_sparse_attention(q, k, v, q_idx, k_idx, w_idx, rel_bias):
    B, S, H, Dh = q.shape
    n_blocks = S // Q_BLOCK
    topk = min(TOPK_MAX, S // 4)
    scale = Dh ** -0.5
    idx_scale = IDX_DIM ** -0.5
    key_pos = jnp.arange(S)
    gather = jax.vmap(lambda arr, ids: arr[ids])

    def block(i):
        start = i * Q_BLOCK
        qb = lax.dynamic_slice_in_dim(q, start, Q_BLOCK, axis=1)
        qib = lax.dynamic_slice_in_dim(q_idx, start, Q_BLOCK, axis=1)
        wib = lax.dynamic_slice_in_dim(w_idx, start, Q_BLOCK, axis=1)
        q_pos = start + jnp.arange(Q_BLOCK)
        sc = jnp.einsum('bqhd,bkd->bqhk', qib, k_idx).astype(jnp.float32) * idx_scale
        iscore = jnp.einsum('bqhk,bqh->bqk', jax.nn.relu(sc), wib.astype(jnp.float32))
        causal = key_pos[None, :] <= q_pos[:, None]
        iscore = jnp.where(causal[None], iscore, -jnp.inf)
        _, sel = lax.top_k(iscore, topk)
        kg = gather(k, sel)
        vg = gather(v, sel)
        logits = jnp.einsum('bqhd,bqkhd->bhqk', qb, kg).astype(jnp.float32) * scale
        dist = q_pos[None, :, None] - sel
        valid = dist >= 0
        bias = rel_bias[t5_bucket(dist)].astype(jnp.float32)
        logits = logits + jnp.transpose(bias, (0, 3, 1, 2))
        logits = jnp.where(valid[:, None], logits, -jnp.inf)
        p = jax.nn.softmax(logits, axis=-1).astype(vg.dtype)
        return jnp.einsum('bhqk,bqkhd->bqhd', p, vg)

    out = lax.map(block, jnp.arange(n_blocks))
    return jnp.transpose(out, (1, 0, 2, 3, 4)).reshape(B, S, H, Dh)

def first_inputs(seed: int = 0) -> dict:
    key = jax.random.key(seed)
    ks = jax.random.split(key, 16)
    D = D_MODEL
    nrm = lambda k, shape, s: jax.random.normal(k, shape, jnp.float32) * s
    return {
        "x": nrm(ks[0], (BATCH, SEQ, D), 1.0),
        "c": nrm(ks[1], (BATCH, D), 1.0),
        "w_ada": nrm(ks[2], (D, 6 * D), 0.5 * D ** -0.5),
        "b_ada": nrm(ks[3], (6 * D,), 0.02),
        "g_norm1": 1.0 + nrm(ks[4], (D,), 0.02),
        "w_in": nrm(ks[5], (D, D_IN), D ** -0.5),
        "b_forget": nrm(ks[6], (N_FOX_HEADS,), 0.1),
        "rel_bias": nrm(ks[7], (N_BUCKETS, N_DSA_HEADS), 0.5),
        "w_branch_fox": nrm(ks[8], (FOX_W, D), FOX_W ** -0.5),
        "w_branch_dsa": nrm(ks[9], (DSA_W, D), DSA_W ** -0.5),
        "w_out": nrm(ks[10], (D, D), D ** -0.5),
        "g_norm2": 1.0 + nrm(ks[11], (D,), 0.02),
        "w_mlp1": nrm(ks[12], (D, D_FF), D ** -0.5),
        "w_mlp2": nrm(ks[13], (D_FF, D), D_FF ** -0.5),
        "g_final": 1.0 + nrm(ks[14], (D,), 0.02),
    }

def first_block(x, c, w_ada, b_ada, g_norm1, w_in, b_forget, rel_bias, w_branch_fox,
              w_branch_dsa, w_out, g_norm2, w_mlp1, w_mlp2, g_final):
    B, S, D = x.shape
    ada = (c @ w_ada + b_ada)[:, None, :]
    shift1, scale1, gate1, shift2, scale2, gate2 = jnp.split(ada, 6, axis=-1)

    for _ in range(DEPTH):
        h = rmsnorm(x, g_norm1) * (1.0 + scale1) + shift1
        proj = h @ w_in
        (q_f, k_f, v_f, f_logit, q_d, k_d, v_d, q_i, k_i, w_i,
         gate_fox, gate_dsa) = jnp.split(proj, SPLIT_POINTS, axis=-1)
        hs = (B, S, -1, HEAD_DIM)
        log_f = jax.nn.log_sigmoid((f_logit + b_forget).astype(jnp.float32))
        cum_logf = jnp.cumsum(log_f, axis=1)
        y_fox = forgetting_attention(q_f.reshape(hs), k_f.reshape(hs), v_f.reshape(hs),
                                     cum_logf).reshape(B, S, FOX_W)
        w_i = w_i * (N_IDX_HEADS ** -0.5)
        y_dsa = indexer_sparse_attention(
            q_d.reshape(hs), k_d.reshape(hs), v_d.reshape(hs),
            q_i.reshape(B, S, N_IDX_HEADS, IDX_DIM), k_i, w_i, rel_bias
        ).reshape(B, S, DSA_W)
        merged = (jax.nn.sigmoid(gate_fox) * (y_fox @ w_branch_fox)
                  + jax.nn.sigmoid(gate_dsa) * (y_dsa @ w_branch_dsa))
        x = x + gate1 * (merged @ w_out)

        h2 = rmsnorm(x, g_norm2) * (1.0 + scale2) + shift2
        x = x + gate2 * (jnp.square(jax.nn.relu(h2 @ w_mlp1)) @ w_mlp2)

    return rmsnorm(x, g_final)


DEPTH_2 = 2

N_MIXERS = 3
D_FF_2 = 2816
LN_EPS = 1e-5
DEEPNORM_ALPHA = (2 * DEPTH_2) ** 0.25
DEEPNORM_BETA = (8 * DEPTH_2) ** -0.25
A_HEADS = 8
A_HEAD_DIM = D_MODEL // A_HEADS
MOBA_BLOCK = 256
MOBA_TOPK = 3
MOBA_Q_CHUNK = 32
REL_BUCKETS = 32
REL_MAX_EXACT = REL_BUCKETS // 2
REL_MAX_DIST = 128
POOL_WINDOWS = (2, 4, 8, 16)
POOL_GROUP = D_MODEL // len(POOL_WINDOWS)
C_HEADS = 4
C_HEAD_DIM = D_MODEL // C_HEADS
C_CONV = 4
C_CHUNK = 64
N_A = len(range(0, DEPTH_2, N_MIXERS))
N_B = len(range(1, DEPTH_2, N_MIXERS))
N_C = len(range(2, DEPTH_2, N_MIXERS))


def layer_norm(x, g, b):
    xf = x.astype(jnp.float32)
    mu = jnp.mean(xf, axis=-1, keepdims=True)
    var = jnp.mean(jnp.square(xf - mu), axis=-1, keepdims=True)
    y = (xf - mu) * lax.rsqrt(var + LN_EPS)
    return (y * g.astype(jnp.float32) + b.astype(jnp.float32)).astype(x.dtype)

def swiglu(x, w_gu, w_down):
    g, u = jnp.split(x @ w_gu, 2, axis=-1)
    return (jax.nn.silu(g) * u) @ w_down

def t5_bucket_2(dist):
    n = jnp.maximum(dist, 0)
    is_small = n < REL_MAX_EXACT
    nf = jnp.maximum(n, 1).astype(jnp.float32)
    large = REL_MAX_EXACT + (jnp.log(nf / REL_MAX_EXACT) / math.log(REL_MAX_DIST / REL_MAX_EXACT)
                             * (REL_BUCKETS - REL_MAX_EXACT)).astype(jnp.int32)
    large = jnp.minimum(large, REL_BUCKETS - 1)
    return jnp.where(is_small, n, large)

def moba_attention(h, w_in, w_out, rel_bias):
    B, S, _ = h.shape
    H, dh, blk, qcs = A_HEADS, A_HEAD_DIM, MOBA_BLOCK, MOBA_Q_CHUNK
    qkv = (h @ w_in).reshape(B, S, 3, H, dh)
    q, k, v = [jnp.transpose(qkv[:, :, j], (0, 2, 1, 3)) for j in range(3)]
    nb = -(-S // blk)
    pad = nb * blk - S
    kb = jnp.pad(k, ((0, 0), (0, 0), (0, pad), (0, 0))).reshape(B, H, nb, blk, dh)
    vb = jnp.pad(v, ((0, 0), (0, 0), (0, pad), (0, 0))).reshape(B, H, nb, blk, dh)
    q_block = jnp.arange(S) // blk
    n_sel = min(MOBA_TOPK, nb - 1)
    scale = dh ** -0.5
    rel_t = rel_bias.T
    bi = jnp.arange(B)[:, None, None, None]
    hi = jnp.arange(H)[None, :, None, None]
    if n_sel > 0:
        k_mean = jnp.mean(kb.astype(jnp.float32), axis=3)
        gate = jnp.einsum('bhsd,bhnd->bhsn', q.astype(jnp.float32), k_mean)
        past = jnp.arange(nb)[None, :] < q_block[:, None]
        gate = jnp.where(past, gate, -jnp.inf)
        _, top_idx = lax.top_k(gate, n_sel)
        top_valid = top_idx < q_block[:, None]

    def chunk_attend(c):
        start = c * qcs
        qc = lax.dynamic_slice_in_dim(q, start, qcs, axis=2)
        qpos = start + jnp.arange(qcs)
        j = start // blk
        ko = lax.dynamic_index_in_dim(kb, j, axis=2, keepdims=False)
        vo = lax.dynamic_index_in_dim(vb, j, axis=2, keepdims=False)
        kpos = j * blk + jnp.arange(blk)
        dist = qpos[:, None] - kpos[None, :]
        bias_own = jnp.transpose(rel_bias[t5_bucket_2(dist)], (2, 0, 1))
        s_own = jnp.einsum('bhqd,bhkd->bhqk', qc, ko) * scale + bias_own
        s_own = jnp.where(dist >= 0, s_own, -jnp.inf).astype(jnp.float32)
        if n_sel > 0:
            idx = lax.dynamic_slice_in_dim(top_idx, start, qcs, axis=2)
            valid = lax.dynamic_slice_in_dim(top_valid, start, qcs, axis=2)
            kg = kb[bi, hi, idx]
            vg = vb[bi, hi, idx]
            kpos_sel = idx[..., None] * blk + jnp.arange(blk)
            bucket = t5_bucket_2(qpos[:, None, None] - kpos_sel)
            s_sel = jnp.einsum('bhqd,bhqnkd->bhqnk', qc, kg) * scale + rel_t[hi[..., None], bucket]
            s_sel = jnp.where(valid[..., None], s_sel, -jnp.inf).astype(jnp.float32)
            logits = jnp.concatenate([s_own, s_sel.reshape(B, H, qcs, n_sel * blk)], axis=-1)
            p = jax.nn.softmax(logits, axis=-1).astype(v.dtype)
            out = (jnp.einsum('bhqk,bhkd->bhqd', p[..., :blk], vo)
                   + jnp.einsum('bhqnk,bhqnkd->bhqd', p[..., blk:].reshape(B, H, qcs, n_sel, blk), vg))
        else:
            p = jax.nn.softmax(s_own, axis=-1).astype(v.dtype)
            out = jnp.einsum('bhqk,bhkd->bhqd', p, vo)
        return out

    outs = lax.map(chunk_attend, jnp.arange(S // qcs))
    o = jnp.transpose(outs, (1, 0, 3, 2, 4)).reshape(B, S, H * dh)
    return o @ w_out

def pool_mixer(h, w_in, w_group, scale, w_out):
    B, S, _ = h.shape
    u = h @ w_in
    counts = jnp.arange(1, S + 1, dtype=jnp.float32)
    pooled = []
    for g, w in enumerate(POOL_WINDOWS):
        ug = u[..., g * POOL_GROUP:(g + 1) * POOL_GROUP].astype(jnp.float32)
        cs = jnp.cumsum(ug, axis=1)
        cs_lag = jnp.pad(cs, ((0, 0), (w, 0), (0, 0)))[:, :S]
        mean = (cs - cs_lag) / jnp.minimum(counts, float(w))[:, None]
        pooled.append(mean - ug)
    p = jnp.stack(pooled, axis=2).astype(h.dtype)
    y = jnp.einsum('bsgc,gcd->bsgd', p, w_group).reshape(B, S, D_MODEL) * scale
    return y @ w_out

def causal_conv(x, w):
    S = x.shape[1]
    xp = jnp.pad(x, ((0, 0), (C_CONV - 1, 0), (0, 0)))
    y = w[0] * xp[:, 0:S]
    for j in range(1, C_CONV):
        y = y + w[j] * xp[:, j:j + S]
    return y

def mlstm_chunkwise(q, k, v, i_pre, log_f):
    B, H, S, dh = q.shape
    L = C_CHUNK
    nc = S // L

    def to_chunks(t):
        return jnp.moveaxis(t.reshape((B, H, nc, L) + t.shape[3:]), 2, 0)

    qc, kc, vc, ic = to_chunks(q), to_chunks(k), to_chunks(v), to_chunks(i_pre)
    bc = jnp.cumsum(to_chunks(log_f), axis=-1)
    causal = jnp.tril(jnp.ones((L, L), dtype=bool))

    def step(carry, xs):
        C, n, m = carry
        qx, kx, vx, ix, bx = xs
        d_intra = jnp.where(causal, bx[..., :, None] - bx[..., None, :] + ix[..., None, :], -jnp.inf)
        m_inter = bx + m[..., None]
        m_t = jnp.maximum(m_inter, jnp.max(d_intra, axis=-1))
        w = jnp.exp(d_intra - m_t[..., None]) * jnp.einsum('bhtd,bhsd->bhts', qx, kx)
        s_inter = jnp.exp(m_inter - m_t)
        num = s_inter[..., None] * jnp.einsum('bhtk,bhkv->bhtv', qx, C) + jnp.einsum('bhts,bhsv->bhtv', w, vx)
        den = s_inter * jnp.einsum('bhtk,bhk->bht', qx, n) + jnp.sum(w, axis=-1)
        h = num / jnp.maximum(jnp.abs(den), jnp.exp(-m_t))[..., None]
        b_last = bx[..., -1]
        g = b_last[..., None] - bx + ix
        m_new = jnp.maximum(b_last + m, jnp.max(g, axis=-1))
        decay = jnp.exp(b_last + m - m_new)
        wk = jnp.exp(g - m_new[..., None])
        C = decay[..., None, None] * C + jnp.einsum('bhsk,bhsv->bhkv', kx * wk[..., None], vx)
        n = decay[..., None] * n + jnp.einsum('bhs,bhsk->bhk', wk, kx)
        return (C, n, m_new), h

    init = (jnp.zeros((B, H, dh, dh), jnp.float32), jnp.zeros((B, H, dh), jnp.float32),
            jnp.zeros((B, H), jnp.float32))
    _, hs = lax.scan(step, init, (qc, kc, vc, ic, bc))
    return jnp.moveaxis(hs, 0, 2).reshape(B, H, S, dh)

def mlstm_mixer(h, w_in, b_gates, conv_w, norm_g, w_out):
    B, S, _ = h.shape
    H, dh, D = C_HEADS, C_HEAD_DIM, D_MODEL
    proj = h @ w_in
    qk = jax.nn.silu(causal_conv(proj[..., :2 * D], conv_w))
    v = proj[..., 2 * D:3 * D]
    o_pre = proj[..., 3 * D:4 * D]
    gates = (proj[..., 4 * D:] + b_gates).astype(jnp.float32)

    def heads(t):
        return jnp.transpose(t.reshape(B, S, H, dh).astype(jnp.float32), (0, 2, 1, 3))

    i_pre = jnp.transpose(gates[..., :H], (0, 2, 1))
    log_f = jnp.transpose(jax.nn.log_sigmoid(gates[..., H:]), (0, 2, 1))
    ht = mlstm_chunkwise(heads(qk[..., :D]), heads(qk[..., D:]) * dh ** -0.5, heads(v), i_pre, log_f)
    ht = jnp.transpose(ht, (0, 2, 1, 3))
    hc = jax.nn.sigmoid(o_pre.astype(jnp.float32)).reshape(B, S, H, dh) * ht
    mu = jnp.mean(hc, axis=-1, keepdims=True)
    var = jnp.mean(jnp.square(hc - mu), axis=-1, keepdims=True)
    hn = ((hc - mu) * lax.rsqrt(var + LN_EPS)).reshape(B, S, D) * norm_g.astype(jnp.float32)
    return hn.astype(h.dtype) @ w_out

def second_inputs(seed: int = 0) -> dict:
    key = jax.random.key(seed)
    ks = jax.random.split(key, 18)
    D, H, GC = D_MODEL, C_HEADS, POOL_GROUP

    def nrm(k, shape, std):
        return jax.random.normal(k, shape, jnp.float32) * std

    x = nrm(ks[0], (BATCH, SEQ, D), 1.0)
    rel_bias = nrm(ks[1], (REL_BUCKETS, A_HEADS), 0.2)
    ln_g = 1.0 + nrm(ks[2], (DEPTH_2, 3, D), 0.02)
    ln_b = nrm(ks[3], (DEPTH_2, 3, D), 0.02)
    ffn_w_gu = nrm(ks[4], (DEPTH_2, 2, D, 2 * D_FF_2), D ** -0.5)
    ffn_w_down = nrm(ks[5], (DEPTH_2, 2, D_FF_2, D), D_FF_2 ** -0.5 * DEEPNORM_BETA)
    a_w_in = nrm(ks[6], (N_A, D, 3 * D), D ** -0.5)
    a_w_out = nrm(ks[7], (N_A, D, D), D ** -0.5 * DEEPNORM_BETA)
    b_w_in = nrm(ks[8], (N_B, D, D), D ** -0.5)
    b_w_group = nrm(ks[9], (N_B, len(POOL_WINDOWS), GC, GC), GC ** -0.5)
    b_scale = 1.0 + nrm(ks[10], (N_B, D), 0.1)
    b_w_out = nrm(ks[11], (N_B, D, D), D ** -0.5 * DEEPNORM_BETA)
    c_w_in = nrm(ks[12], (N_C, D, 4 * D + 2 * H), D ** -0.5)
    c_b_gates = jnp.concatenate([nrm(ks[13], (N_C, H), 0.1),
                                 jnp.linspace(3.0, 6.0, H, dtype=jnp.float32)[None, :] + nrm(ks[14], (N_C, H), 0.1)],
                                axis=-1)
    c_conv_w = nrm(ks[15], (N_C, C_CONV, 2 * D), C_CONV ** -0.5)
    c_norm_g = 1.0 + nrm(ks[16], (N_C, D), 0.02)
    c_w_out = nrm(ks[17], (N_C, D, D), D ** -0.5 * DEEPNORM_BETA)
    return {"x": x, "rel_bias": rel_bias, "ln_g": ln_g, "ln_b": ln_b,
            "ffn_w_gu": ffn_w_gu, "ffn_w_down": ffn_w_down,
            "a_w_in": a_w_in, "a_w_out": a_w_out,
            "b_w_in": b_w_in, "b_w_group": b_w_group, "b_scale": b_scale, "b_w_out": b_w_out,
            "c_w_in": c_w_in, "c_b_gates": c_b_gates, "c_conv_w": c_conv_w, "c_norm_g": c_norm_g,
            "c_w_out": c_w_out}

def second_block(x, rel_bias, ln_g, ln_b, ffn_w_gu, ffn_w_down, a_w_in, a_w_out,
              b_w_in, b_w_group, b_scale, b_w_out,
              c_w_in, c_b_gates, c_conv_w, c_norm_g, c_w_out):
    for i in range(DEPTH_2):
        x = layer_norm(DEEPNORM_ALPHA * x + 0.5 * swiglu(x, ffn_w_gu[i, 0], ffn_w_down[i, 0]),
                       ln_g[i, 0], ln_b[i, 0])
        kind, j = i % N_MIXERS, i // N_MIXERS
        if kind == 0:
            y = moba_attention(x, a_w_in[j], a_w_out[j], rel_bias)
        elif kind == 1:
            y = pool_mixer(x, b_w_in[j], b_w_group[j], b_scale[j], b_w_out[j])
        else:
            y = mlstm_mixer(x, c_w_in[j], c_b_gates[j], c_conv_w[j], c_norm_g[j], c_w_out[j])
        x = layer_norm(DEEPNORM_ALPHA * x + y, ln_g[i, 1], ln_b[i, 1])
        x = layer_norm(DEEPNORM_ALPHA * x + 0.5 * swiglu(x, ffn_w_gu[i, 1], ffn_w_down[i, 1]),
                       ln_g[i, 2], ln_b[i, 2])
    return x


def setup_inputs(seed=0):
    out = dict(first_inputs(seed))
    for name, value in second_inputs(seed + 1).items():
        if name != "x":
            out[name + "_2"] = value
    return out


def reference(
    x, c, w_ada, b_ada, g_norm1, w_in, b_forget, rel_bias, w_branch_fox, w_branch_dsa, w_out,
    g_norm2, w_mlp1, w_mlp2, g_final, rel_bias_2, ln_g_2, ln_b_2, ffn_w_gu_2, ffn_w_down_2,
    a_w_in_2, a_w_out_2, b_w_in_2, b_w_group_2, b_scale_2, b_w_out_2, c_w_in_2, c_b_gates_2,
    c_conv_w_2, c_norm_g_2, c_w_out_2,
):
    x = first_block(
        x, c, w_ada, b_ada, g_norm1, w_in, b_forget, rel_bias, w_branch_fox, w_branch_dsa,
        w_out, g_norm2, w_mlp1, w_mlp2, g_final,
    )
    return second_block(
        x, rel_bias_2, ln_g_2, ln_b_2, ffn_w_gu_2, ffn_w_down_2, a_w_in_2, a_w_out_2, b_w_in_2,
        b_w_group_2, b_scale_2, b_w_out_2, c_w_in_2, c_b_gates_2, c_conv_w_2, c_norm_g_2,
        c_w_out_2,
    )


_drawn_inputs = setup_inputs


def setup_inputs(seed=0):
    import zlib

    import numpy as np

    out = dict(_drawn_inputs(seed))
    spreads = {}
    factors = {'g_norm1': 4.212,
     'b_forget': 6.509,
     'g_norm2': 4.159,
     'g_final': 8.031,
     'rel_bias_2': 5.203}
    for name, (base, spread) in spreads.items():
        noise = np.random.default_rng([zlib.crc32(name.encode()), seed]).standard_normal(out[name].shape)
        drawn = base * np.exp(spread * noise) if base else spread * noise
        out[name] = __import__('jax').numpy.asarray(drawn.astype(out[name].dtype))
    for name, factor in factors.items():
        out[name] = (out[name] * factor).astype(out[name].dtype)
    return out
```

```python
from contextlib import ExitStack

import numpy as np

import concourse.bass as bass
from concourse import mybir

P = 128
TOK = 2
D = 1024
KT = D // P
HALF = 512
F32 = mybir.dt.float32
F32R = mybir.dt.float32r
ALU = mybir.AluOpType
ACT = mybir.ActivationFunctionType
AX = mybir.AxisListType

FOX = 512
DSA = 512
NF = 8
DH = 64
NI = 4
TOPK = 64
D_IN = 3 * FOX + NF + 3 * DSA + NI * DH + DH + NI + 2 * D
OFF_F = 3 * FOX
OFF_D = OFF_F + NF
OFF_I = OFF_D + 3 * DSA
N_I = NI * DH + DH + NI
OFF_G = OFF_I + N_I
MISC = N_I + NF
DFF = 4 * D
DFF2 = 2816
GC = 256
NB = 32
MH = 8
ALPHA = 4 ** 0.25
EPS = 1e-6
LN_EPS = 1e-5
MASKED = -1e30
TAKEN = -3e38
WINDOWS = (2, 4, 8, 16)
CONSTANTS = 9
REV = 384
TABW = 256


def weight_units():
    units = []

    def add(name, kind, width, kts):
        units.append((name, kind, width, kts))

    add(("misc",), "wide", MISC, KT)
    for n in ("qd", "kd", "vd", "qf", "kf", "vf"):
        add((n,), "wide", HALF, KT)
    for g in range(4):
        add(("gate", g), "wide", HALF, KT)
    add(("br", 0), "deep", D, 4)
    add(("br", 1), "deep", D, 4)
    for g in range(2):
        add(("wout", g), "deep", D, 4)
    for part in range(2):
        for g in range(4):
            add(("up", 4 * part + g), "wide", HALF, KT)
        for g in range(4):
            add(("down", 4 * part + g), "deep", D, 4)

    def ffn(f):
        for c in range(8):
            add(("gu", f, c), "wide", HALF, KT)
        for g in range(4):
            add(("dn", f, g), "deep", D, 4)
        for c in range(8, 11):
            add(("gu", f, c), "wide", HALF, KT)
        add(("dn", f, 4), "deep", D, 2)
        add(("dn", f, 5), "deep", D, 4)

    ffn(0)
    for c in (0, 2, 4, 1, 3, 5):
        add(("moba", c), "wide", HALF, KT)
    for g in range(2):
        add(("aout", g), "deep", D, 4)
    ffn(1)
    ffn(2)
    for g in range(2):
        add(("bin", g), "deep", D, 4)
    add(("grp",), "deep", HALF, 4)
    for g in range(2):
        add(("bout", g), "deep", D, 4)
    ffn(3)
    return units


UNITS = weight_units()
UNIT = {u[0]: i for i, u in enumerate(UNITS)}


def psum_turns():
    keys = [("tab", 0)] + [("ada", c) for c in range(4)]

    def chain(n):
        keys.extend((n, t, h) for t in range(TOK) for h in range(2))

    chain("h")
    keys.extend([("qi", 0), ("qi", 1), ("qd", 0), ("F",), ("qd", 1), ("kd", 0), ("kd", 1),
                 ("qf", 0), ("qf", 1), ("kf", 0), ("kf", 1)])
    chain("y")
    chain("m")
    keys.extend(("ada", c) for c in range(4, 12))
    chain("c1")
    keys.extend(("up", g, t) for g in range(8) for t in range(TOK))
    chain("c2")

    def ffn(f):
        keys.extend(("gu", f, c, t) for c in range(11) for t in range(TOK))
        chain(("f", f))

    ffn(0)
    keys.append(("tab", 1))
    keys.extend(("moba", c, t) for c in (0, 2, 1, 3) for t in range(TOK))
    chain("my")
    chain("c3")
    ffn(1)
    ffn(2)
    keys.extend(("pool", j) for j in range(4))
    chain("g")
    chain("c4")
    keys.extend(("gu", 3, c, t) for c in range(11) for t in range(TOK))
    return {k: i for i, k in enumerate(keys)}


TURN = psum_turns()
PLAIN = {"tab", "ada", "qi", "qd", "F", "kd", "qf", "kf", "moba"}
BY_SCALAR = {"qi", "qd", "kd", "qf", "kf", "moba"}


def counts(chosen):
    n, out = 0, {}
    for k in TURN:
        if chosen(k):
            n += 1
            out[k] = n
    return out


SPLIT_NO = counts(lambda k: k[0] not in PLAIN)
TMP_S = counts(lambda k: k[0] in BY_SCALAR)
TMP_V = counts(lambda k: k[0] not in BY_SCALAR and k[0] not in ("tab", "ada", "F", "pool", "y", "my"))
TG_NO = counts(lambda k: k[0] in ("up", "gu"))
TG_READ = {}
_last = [0, 0]
for _k in TG_NO:
    TG_READ[_k] = _last[_k[-1]]
    _last[_k[-1]] = TMP_V[_k]


def key_kt(key):
    return 4 * (key[1] % 4) if key[0] == "up" else 2 * (key[2] % 8)


ITEMS = [("d", h) for h in range(NF)] + [("f", h) for h in range(NF)] + [("m", h) for h in range(MH)]
DEEP = {n: i for i, n in enumerate(["br0", "br1", "wout", "mlp", "f0", "aout", "f1", "f2", "bout", "f3"])}
CHAIN = {n: i for i, n in enumerate(["h", "c1", "c2", ("f", 0), "c3", ("f", 1), ("f", 2), "c4", ("f", 3)])}


def build(nc, t, out):
    with ExitStack() as ctx:
        def sb(name, shape, dt=F32):
            return ctx.enter_context(nc.sbuf_tensor(name, shape, dt))

        def bank(name):
            return ctx.enter_context(nc.psum_tensor(name, [P, HALF], F32))

        def sem(name):
            return ctx.enter_context(nc.semaphore(name))

        RAW = sb("RAW", [P, 2, 2048])
        WH = sb("WH", [P, 2, 4096], F32R)
        WL = sb("WL", [P, 2, 4096], F32R)
        AH = sb("AH", [P, KT, 256], F32R)
        AL = sb("AL", [P, KT, 256], F32R)
        hid_at = (nc.sbuf_base + 31) // 32 * 32
        HH = sb("HH", [P, 16, 256], F32R)
        HL = sb("HL", [P, 16, 256], F32R)
        X = sb("X", [P, TOK, D])
        Z = sb("Z", [P, TOK, D])
        ROWS = sb("ROWS", [P, 2, D])
        TAB = sb("TAB", [P, 8, TABW])
        ADA = sb("ADA", [P, 4, D])
        PIECE = sb("PIECE", [P, 2, D])
        TMP = sb("TMP", [P, 2, HALF])
        TG = sb("TG", [P, TOK, HALF])
        PR = sb("PR", [P, 2, REV])
        PT = sb("PT", [P, 2, REV])
        SELM = sb("SELM", [P, REV], F32R)
        CMR = sb("CMR", [P, TABW], F32R)
        IDR = sb("IDR", [P, P], F32R)
        IDENT = sb("IDENT", [P, P])
        TRI = sb("TRI", [P, P])
        ONES = sb("ONES", [P, P])
        CM = sb("CM", [P, TABW])
        FT = sb("FT", [NF, 256])
        FTN = sb("FTN", [NF, 256])
        REL = sb("REL", [64, 8])
        CC = sb("CC", [P, KT])
        BF = sb("BF", [P, NF])
        WI = sb("WI", [P, TOK, NI])
        LF = sb("LF", [P, TOK, 3, NF])
        LFS = sb("LFS", [P, TOK, NF])
        M8 = sb("M8", [P, 8])
        ST = sb("ST", [P, TOK, 12])
        MV = sb("MV", [P, TOK, 2])
        VAR = sb("VAR", [P, TOK])
        RS = sb("RS", [P, TOK])
        NHALF = sb("NHALF", [P, 1])
        NM = sb("NM", [P, 2, 2])
        SM = sb("SM", [P, 2, 2])
        RC = sb("RC", [P, 2, 2])
        ONEHOT = sb("ONEHOT", [NB + 1, REV])

        def over(name, shape, at):
            return nc.alloc_sbuf_tensor_at(name, shape, F32, offset=hid_at + at)

        WADA = over("WADA", [P, 4, 2 * D], 0)
        QD, KD, QF, KF = (over(n, [P, 4, 256], 4096 * i) for i, n in enumerate(("QD", "KD", "QF", "KF")))
        SIG = over("SIG", [P, TOK, 2 * D], 16384)
        QM = over("QM", [P, MH, 256], 0)
        KM = over("KM", [P, MH, 256], 8192)
        VM = over("VM", [P, TOK, D], 16384)
        YM = over("YM", [P, TOK, D], 24576)
        UU = over("UU", [P, TOK, D], 8192)
        POOLM = over("POOLM", [P, 4, TOK, 256], 24576)
        QI = PT[:, :, :].rearrange("p a b -> p (a b)")[:, 0:512].rearrange("p (a b) -> p a b", a=2)
        KI = PT[:, 1, 128:384]
        REVROW = PR[0:8, 1, :]
        VD = Z[:, :, 0:512]
        VF = Z[:, :, 512:1024]
        YA = ROWS
        REVD = nc.dram_tensor("rev_rows", [2, P, 8, REV], F32, kind="Internal").ap()

        UP = [bank(f"UP{i}") for i in range(TOK)]
        Y = [[bank(f"Y{i}{h}") for h in range(2)] for i in range(TOK)]
        TB = [bank(f"TB{i}") for i in range(2)]
        SB = Y[0]
        PTB = Y[1][0]
        OB = Y[1][1]
        IDX = [Y[0][0], Y[0][1], Y[1][0], Y[1][1]]

        raw_in = [sem("raw_in0"), sem("raw_in1")]
        wh_done = sem("wh_done")
        wl_done = sem("wl_done")
        mm_done = sem("mm_done")
        up_copied = sem("up_copied")
        y_free = [sem("y_free0"), sem("y_free1")]
        tmp_s = sem("tmp_s")
        tmp_v = sem("tmp_v")
        tr_done = sem("tr_done")
        th_done = sem("th_done")
        tr_free = [sem("tr_free0"), sem("tr_free1")]
        tg_done = sem("tg_done")
        s_done = sem("s_done")
        m_done = sem("m_done")
        p_done = sem("p_done")
        pt_tr = sem("pt_tr")
        pt_cp = sem("pt_cp")
        pv_done = sem("pv_done")
        y_done = sem("y_done")
        rc_done = sem("rc_done")
        idx_done = sem("idx_done")
        r_done = sem("r_done")
        r_used = sem("r_used")
        cmr_done = sem("cmr_done")
        sel_done = sem("sel_done")
        lf_in = sem("lf_in")
        lf_mid = sem("lf_mid")
        lf_done = sem("lf_done")
        sig_done = sem("sig_done")
        var_done = sem("var_done")
        rs_done = sem("rs_done")
        v_seq = sem("v_seq")
        s_seq = sem("s_seq")
        g_seq = sem("g_seq")
        in_x = sem("in_x")
        in_c = sem("in_c")
        in_wada = [sem(f"in_wada{i}") for i in range(4)]
        wada_used = sem("wada_used")
        in_piece = [sem("in_piece0"), sem("in_piece1")]
        piece_used = sem("piece_used")
        in_brow = sem("in_brow")
        in_rows = sem("in_rows")
        rev_out = sem("rev_out")
        in_tab = sem("in_tab")
        uu_done = sem("uu_done")
        in_pool = sem("in_pool")
        out_ready = sem("out_ready")
        out_done = sem("out_done")

        block = ctx.enter_context(nc.Block())

        def taps(u, tile_end):
            _, _, width, kts = UNITS[u]
            quarter = width * kts // 4
            return 4 * u + (tile_end + quarter - 1) // quarter

        up_read = {}
        copies = 0
        for u, (name, kind, _, _) in enumerate(UNITS):
            for tok in range(TOK if kind == "wide" else 0):
                k = name[0]
                if k == "misc":
                    up_read[u, tok] = (lf_done, tok + 1)
                elif k in ("vd", "vf", "gate") or (k == "moba" and name[1] >= 4):
                    copies += 1
                    up_read[u, tok] = (up_copied, copies)
                elif k in BY_SCALAR:
                    up_read[u, tok] = (tmp_s, TMP_S[name + (tok,)])
                elif k == "up":
                    up_read[u, tok] = (tg_done, TG_NO[name + (tok,)])
                else:
                    up_read[u, tok] = (tmp_v, TMP_V[name + (tok,)])
        wides = [u for u, unit in enumerate(UNITS) if unit[1] == "wide"]
        wide_before = dict(zip(wides[1:], wides))

        def emptied(b):
            return tr_free[b % 2], b // 2 + 1

        def item_views(a):
            kind, h = ITEMS[a]
            if kind == "m":
                return (QM[:, h, :], KM[:, h, :], VM[:, :, h * P:(h + 1) * P], YM[:, :, h * P:(h + 1) * P], P)
            q, k, v = (QD, KD, VD) if kind == "d" else (QF, KF, VF)
            o = 0 if kind == "d" else 512
            rows = slice(64 * (h % 2), 64 * (h % 2) + 64)
            return (q[rows, h // 2, :], k[rows, h // 2, :], v[:, :, h * DH:(h + 1) * DH],
                    YA[:, :, o + h * DH:o + (h + 1) * DH], DH)

        @block.sync
        def _(sp):
            gu, dn = t["ffn_w_gu_2"], t["ffn_w_down_2"]

            def src(name):
                k = name[0]
                i, j = (name[1] // 2, name[1] % 2) if k in ("gu", "dn") else (0, 0)
                return {
                    "qd": lambda: (t["w_in"], OFF_D), "kd": lambda: (t["w_in"], OFF_D + DSA),
                    "vd": lambda: (t["w_in"], OFF_D + 2 * DSA), "qf": lambda: (t["w_in"], 0),
                    "kf": lambda: (t["w_in"], FOX), "vf": lambda: (t["w_in"], 2 * FOX),
                    "gate": lambda: (t["w_in"], OFF_G + name[1] * HALF),
                    "br": lambda: ((t["w_branch_dsa"], t["w_branch_fox"])[name[1]], 0),
                    "wout": lambda: (t["w_out"], 0), "up": lambda: (t["w_mlp1"], name[1] * HALF),
                    "down": lambda: (t["w_mlp2"], 0), "gu": lambda: (gu[i, j], name[2] * GC),
                    "dn": lambda: (dn[i, j], 0), "moba": lambda: (t["a_w_in_2"][0], name[1] * HALF),
                    "aout": lambda: (t["a_w_out_2"][0], 0), "bin": lambda: (t["b_w_in_2"][0], 0),
                    "bout": lambda: (t["b_w_out_2"][0], 0),
                }[k]()

            sp.dma_start(X[:, :, :], t["x"][0].rearrange("(a p) n -> p a n", p=P)).then_inc(in_x, 16)
            wada = t["w_ada"].rearrange("(p k) n -> p k n", k=KT)
            for k in range(4):
                sp.dma_start(WADA[:, k, :], wada[:, k, 0:2 * D]).then_inc(in_wada[k], 16)
            for k in range(4, KT):
                sp.wait_ge(wada_used, k - 3)
                sp.dma_start(WADA[:, k % 4, :], wada[:, k, 0:2 * D]).then_inc(in_wada[k % 4], 16)

            for u, (name, kind, width, kts) in enumerate(UNITS):
                for half in range(2):
                    if u:
                        sp.wait_ge(wl_done, 4 * u - 2 + 2 * half)
                    n = width * kts // 2
                    dst = RAW[:, half, 0:n]
                    if name[0] == "misc":
                        w = t["w_in"].rearrange("(k p) n -> p k n", p=P)[:, 4 * half:4 * half + 4, :]
                        d = dst.rearrange("p (k n) -> p k n", k=4)
                        parts = [(d[:, :, 0:N_I], w[:, :, OFF_I:OFF_I + N_I]),
                                 (d[:, :, N_I:MISC], w[:, :, OFF_F:OFF_F + NF])]
                    elif name[0] == "grp":
                        w = t["b_w_group_2"][0]
                        parts = [(dst[:, 512 * g:512 * g + 512].rearrange("p (k n) -> p k n", k=2),
                                  w[2 * half + g].rearrange("(k p) n -> p k n", p=P)) for g in range(2)]
                    elif name[0] == "gu":
                        m, c = src(name)
                        w = m.rearrange("(k p) n -> p k n", p=P)[:, 4 * half:4 * half + 4, :]
                        d = dst.rearrange("p (k g n) -> p k g n", k=4, g=2)
                        parts = [(d[:, :, g, :], w[:, :, g * DFF2 + c:g * DFF2 + c + GC]) for g in range(2)]
                    elif kind == "wide":
                        m, c = src(name)
                        w = m.rearrange("(k p) n -> p k n", p=P)
                        d = dst.rearrange("p (k n) -> p k n", k=4)
                        parts = [(d[:, 2 * g:2 * g + 2, :],
                                  w[:, 4 * half + 2 * g:4 * half + 2 * g + 2, c:c + HALF]) for g in range(2)]
                    else:
                        m, _ = src(name)
                        k0 = {("dn", 5): 18}.get((name[0], name[-1]), 0 if name[0] == "br" else 4 * name[-1])
                        k0 += (kts // 2) * half
                        w = m.rearrange("(k p) n -> p k n", p=P)
                        d = dst.rearrange("p (k n) -> p k n", n=D)
                        if kts == 4:
                            parts = [(d[:, g, :], w[:, k0 + g, :]) for g in range(2)]
                        else:
                            parts = [(d[:, 0, 512 * g:512 * g + 512], w[:, k0, 512 * g:512 * g + 512])
                                     for g in range(2)]
                    for dd, ss in parts:
                        sp.dma_start(dd, ss).then_inc(raw_in[half], 16)
            for tok in range(TOK):
                sp.wait_ge(out_ready, tok + 1)
                sp.dma_start(out[0, tok * P:(tok + 1) * P, :], X[:, tok, :]).then_inc(out_done, 16)
            sp.wait_ge(out_done, 16 * TOK)

        @block.gpsimd
        def _(gp):
            seq = [0]

            def step(ins):
                seq[0] += 1
                ins.then_inc(g_seq, 1)
                gp.wait_ge(g_seq, seq[0])

            gp.dma_start(CC[:, :], t["c"][0].rearrange("(p k) -> p k", k=KT)).then_inc(in_c, 16)
            gp.dma_start(BF[:, :], t["b_forget"].partition_broadcast(P)).then_inc(in_c, 16)
            gp.dma_start(REL[0:NB, :], t["rel_bias"]).then_inc(in_c, 16)
            gp.dma_start(ONEHOT[:, :], t["onehot"]).then_inc(in_c, 16)
            gp.dma_start(ROWS[:, 0, :], t["g_norm1"].partition_broadcast(P)).then_inc(in_rows, 16)
            step(gp.memset(ADA[:, 0:2, :], 0.0))
            gp.dma_start(ADA[0:1, 0:2, :], t["b_ada"][0:2 * D].rearrange("(o a n) -> o a n", o=1, a=2)
                         ).then_inc(in_brow, 16)
            step(gp.memset(REL[NB:NB + 1, :], MASKED))
            step(gp.memset(NHALF[:, :], -0.5))
            step(gp.memset(ONES[:, :], 1.0))
            step(gp.memset(IDENT[:, :], 0.0))
            step(gp.affine_select(out=IDENT[:, :], in_=IDENT[:, :], compare_op=ALU.not_equal, fill=1.0, base=0,
                                  pattern=[[-1, P]], channel_multiplier=1))
            step(gp.affine_select(out=TRI[:, :], in_=ONES[:, :], compare_op=ALU.is_ge, fill=0.0, base=0,
                                  pattern=[[1, P]], channel_multiplier=-1))
            step(gp.memset(CM[:, :], 0.0))
            step(gp.affine_select(out=CM[:, :], in_=CM[:, :], compare_op=ALU.is_ge, fill=MASKED, base=P,
                                  pattern=[[-1, TABW]], channel_multiplier=1))
            assert seq[0] == CONSTANTS

            def table(n):
                gp.wait_ge(*emptied(TURN[("tab", n)]))
                gp.dma_start(REVD[n].rearrange("c h x -> h c x"),
                             REVROW[:, :].unsqueeze(1).to_broadcast([8, P, REV])).then_inc(rev_out, 16)
                gp.wait_ge(rev_out, 16 * (n + 1))
                start = REVD[n, 0, 0, P - 1:P]
                gp.dma_start(TAB[:, :, :], bass.AP(start.tensor, start.offset, [[8 * REV - 1, P], [REV, 8], [1, TABW]])
                             ).then_inc(in_tab, 16)

            def rsqrt(n, eps):
                for tok in range(TOK):
                    gp.wait_ge(var_done, 2 * n + tok + 1)
                    step(gp.tensor_scalar(VAR[:, tok:tok + 1], VAR[:, tok:tok + 1], eps, 1.0, ALU.add, ALU.mult))
                    gp.tensor_tensor(RS[:, tok:tok + 1], VAR[:, tok:tok + 1], NHALF[:, :], ALU.pow
                                     ).then_inc(rs_done, 1)
                    gp.wait_ge(rs_done, 2 * n + tok + 1)

            rsqrt(0, EPS)
            table(0)
            gp.wait_ge(tmp_v, TMP_V[("h", 1, 1)])
            step(gp.memset(ADA[:, :, :], 0.0))
            gp.dma_start(ADA[0:1, :, :], t["b_ada"][2 * D:6 * D].rearrange("(o a n) -> o a n", o=1, a=4)
                         ).then_inc(in_brow, 16)
            wada = t["w_ada"].rearrange("(p k) n -> p k n", k=KT)
            for i in range(32):
                if i >= 2:
                    gp.wait_ge(piece_used, i - 1)
                gp.dma_start(PIECE[:, i % 2, :], wada[:, i % KT, 2 * D + (i // KT) * D:3 * D + (i // KT) * D]
                             ).then_inc(in_piece[i % 2], 16)
            gp.wait_ge(tr_done, TURN[("y", 1, 1)] + 1)
            gp.dma_start(ROWS[:, 0, :], t["g_norm2"].partition_broadcast(P)).then_inc(in_rows, 16)
            gp.dma_start(ROWS[:, 1, :], t["g_final"].partition_broadcast(P)).then_inc(in_rows, 16)
            rsqrt(1, EPS)
            rsqrt(2, EPS)

            def rows(before, layer, j):
                gp.wait_ge(tmp_v, TMP_V[(before, 1, 1)])
                gp.dma_start(ROWS[:, 0, :], t["ln_g_2"][layer, j].partition_broadcast(P)).then_inc(in_rows, 16)
                gp.dma_start(ROWS[:, 1, :], t["ln_b_2"][layer, j].partition_broadcast(P)).then_inc(in_rows, 16)

            rows("c2", 0, 0)
            gp.wait_ge(y_done, 2 * NF)
            gp.dma_start(REL[0:NB, :], t["rel_bias_2"]).then_inc(in_c, 16)
            rsqrt(3, LN_EPS / ALPHA ** 2)
            table(1)
            rows(("f", 0), 0, 1)
            rsqrt(4, LN_EPS / ALPHA ** 2)
            rows("c3", 0, 2)
            rsqrt(5, LN_EPS / ALPHA ** 2)
            rows(("f", 1), 1, 0)
            gp.dma_start(ADA[:, 0, :], t["b_scale_2"][0].partition_broadcast(P)).then_inc(in_pool, 16)
            rsqrt(6, LN_EPS / ALPHA ** 2)
            gp.wait_ge(mm_done, 2 * UNIT[("dn", 2, 5)] + 2)
            gp.dma_start(POOLM[:, :, :, :], t["pool_m"]).then_inc(in_pool, 16)
            rows(("f", 2), 1, 1)
            rsqrt(7, LN_EPS / ALPHA ** 2)
            rows("c4", 1, 2)
            rsqrt(8, LN_EPS / ALPHA ** 2)

        @block.tensor
        def _(pe):
            def three(dst, ah, al, wh, wl, first, last):
                pe.matmul(dst, ah, wh, start=first, stop=False)
                pe.matmul(dst, ah, wl, start=False, stop=False)
                return pe.matmul(dst, al, wh, start=False, stop=last)

            def quarters(u, tok, end):
                if tok == 0:
                    pe.wait_ge(wl_done, taps(u, end))

            def wide(u, tok):
                _, _, width, kts = UNITS[u]
                if u in wide_before:
                    pe.wait_ge(*up_read[wide_before[u], tok])
                ts = slice(tok * P, (tok + 1) * P)
                for k in range(kts):
                    quarters(u, tok, (k + 1) * width)
                    w = slice(k * width, (k + 1) * width)
                    mm = three(UP[tok][:, 0:width], AH[:, k, ts], AL[:, k, ts], WH[:, u % 2, w], WL[:, u % 2, w],
                               k == 0, k == kts - 1)
                mm.then_inc(mm_done, 1)

            def deep(u, tok, ah, al, k0, first, last, product):
                kts = UNITS[u][3]
                ts = slice(tok * P, (tok + 1) * P)
                if first and DEEP.get(product):
                    pe.wait_ge(y_free[tok], DEEP[product])
                for k in range(kts):
                    for h in range(2):
                        o = k * D + h * HALF
                        quarters(u, tok, o + HALF)
                        w = slice(o, o + HALF)
                        mm = three(Y[tok][h][:, :], ah[:, k0 + k, ts], al[:, k0 + k, ts], WH[:, u % 2, w],
                                   WL[:, u % 2, w], first and k == 0, last and k == kts - 1)
                mm.then_inc(mm_done, 1)

            def bank_of(key):
                b = TURN[key]
                if b >= 2:
                    pe.wait_ge(*emptied(b - 2))
                return TB[b % 2]

            def turn(key, blocks, source):
                dst = bank_of(key)
                if key in TMP_S:
                    pe.wait_ge(tmp_s, TMP_S[key])
                elif key in TMP_V:
                    pe.wait_ge(tmp_v, TMP_V[key])
                for i in range(blocks):
                    mm = pe.transpose(dst[:, i * P:(i + 1) * P], source[:, i * P:(i + 1) * P], IDENT[:, :])
                mm.then_inc(tr_done, 1)

            def from_tmp(key, blocks):
                turn(key, blocks, TMP[:, TURN[key] % 2, :])

            def chain_turns(name, tok, buf):
                for h in range(2):
                    turn((name, tok, h), 4, buf[:, tok, h * HALF:(h + 1) * HALF])

            def ready(key):
                pe.wait_ge(*emptied(TURN[key]))

            def score(a):
                kind, h = ITEMS[a]
                q, k, _, _, _ = item_views(a)
                if h == 0 or (kind, h) == ("m", 4):
                    ready({"d": ("kd", 1), "f": ("kf", 1), "m": ("moba", 2 + h // 4, 1)}[kind])
                if a == 0:
                    pe.wait_ge(sel_done, 1)
                if a >= 2:
                    pe.wait_ge(p_done, a - 1)
                last = kind == "m"
                for lo, hi, ql, n in ((0, P, 0, P), (P, REV, P, 256)):
                    dst = SB[a % 2][:, lo:hi]
                    mm = pe.matmul(dst, q[:, ql:ql + P], k[:, 0:n], start=True, stop=last)
                    if kind == "f":
                        pick = IDENT[0:NF, h:h + 1]
                        pe.matmul(dst, pick.to_broadcast([NF, P]), FTN[:, 0:n], start=False, stop=False)
                        pe.matmul(dst, FT[:, ql:ql + P], pick.to_broadcast([NF, n]), start=False, stop=False)
                    if kind != "m":
                        mask = CMR[:, 256 - n:256] if kind == "f" else SELM[:, lo:hi]
                        mm = pe.matmul(dst, IDR[:, :], mask, start=False, stop=True)
                mm.then_inc(s_done, 1)

            def turn_probs(a):
                pe.wait_ge(p_done, a + 1)
                if a:
                    pe.wait_ge(pt_cp, a)
                for i in range(3):
                    mm = pe.transpose(PTB[:, i * P:(i + 1) * P], PR[:, a % 2, i * P:(i + 1) * P], IDENT[:, :])
                mm.then_inc(pt_tr, 1)

            def values(a):
                _, _, v, _, dh = item_views(a)
                pe.wait_ge(pt_cp, a + 1)
                if a:
                    pe.wait_ge(y_done, a)
                pt = PT[:, a % 2, :]
                pe.matmul(OB[:, 0:dh], pt[:, 0:P], v[:, 0, :], start=True, stop=True)
                pe.matmul(OB[:, P:P + dh], pt[:, P:2 * P], v[:, 0, :], start=True, stop=False)
                pe.matmul(OB[:, P:P + dh], pt[:, 2 * P:3 * P], v[:, 1, :], start=False, stop=True
                          ).then_inc(pv_done, 1)

            def slot(a, first, end):
                if first < a <= end:
                    turn_probs(a - 1)
                if a < end:
                    score(a)
                if first < a <= end:
                    values(a - 1)

            pe.wait_ge(in_c, 64)
            pe.wait_ge(g_seq, CONSTANTS)
            pe.wait_ge(cmr_done, 1)

            def rev_row(n):
                dst = bank_of(("tab", n))
                pe.matmul(dst[0:8, 0:REV], REL[0:NB + 1, :], ONEHOT[:, :], start=True, stop=True
                          ).then_inc(tr_done, 1)

            def ada_sum(c, col):
                dst = bank_of(("ada", c))
                pe.matmul(dst[:, :], ONES[:, :], ADA[:, col // 2, (col % 2) * HALF:(col % 2 + 1) * HALF],
                          start=True, stop=True).then_inc(tr_done, 1)

            rev_row(0)
            pe.wait_ge(wada_used, KT)
            for c in range(4):
                ada_sum(c, c)
            chain_turns("h", 0, Z)
            att = 0
            late = []
            for u in range(11):
                name = UNITS[u][0]
                if u == 0:
                    ready(("h", 0, 1))
                wide(u, 0)
                if u == 0:
                    chain_turns("h", 1, Z)
                    ready(("h", 1, 1))
                for key, n in late:
                    from_tmp(key, n)
                late = []
                if u >= 4:
                    slot(att, 0, 2 * NF)
                    att += 1
                wide(u, 1)
                if name[0] in ("misc", "qd", "kd", "qf", "kf"):
                    key, n = ("qi", 3) if name[0] == "misc" else (name[0], 4)
                    from_tmp((key, 0), n)
                    late = [((key, 1), n)]
                if u == 1:
                    dst = bank_of(("F",))
                    pe.wait_ge(lf_done, 2)
                    pe.matmul(dst[0:NF, 0:P], LFS[:, 0, :], TRI[:, :], start=True, stop=True)
                    pe.matmul(dst[0:NF, P:256], LFS[:, 1, :], TRI[:, :], start=True, stop=False)
                    pe.matmul(dst[0:NF, P:256], LFS[:, 0, :], ONES[:, :], start=False, stop=True
                              ).then_inc(tr_done, 1)
                    ready(("qi", 1))
                    for h in range(NI):
                        r = slice(64 * (h % 2), 64 * (h % 2) + 64)
                        pe.matmul(IDX[h][:, 0:P], QI[r, h // 2, 0:P], KI[r, 0:P], start=True, stop=True)
                        mm = pe.matmul(IDX[h][:, P:REV], QI[r, h // 2, P:256], KI[r, 0:256],
                                       start=True, stop=True)
                    mm.then_inc(idx_done, 1)
                if u >= 4:
                    slot(att, 0, 2 * NF)
                    att += 1
            while att <= 2 * NF:
                slot(att, 0, 2 * NF)
                att += 1
            pe.wait_ge(y_done, 2 * NF)
            for tok in range(TOK):
                chain_turns("y", tok, YA)
            for b in range(2):
                u = UNIT[("br", b)]
                for tok in range(TOK):
                    ready(("y", tok, b))
                    deep(u, tok, AH, AL, 4 * b, True, True, f"br{b}")
            chain_turns("m", 0, Z)

            u = UNIT[("wout", 0)]
            ready(("m", 0, 1))
            deep(u, 0, AH, AL, 0, True, False, "wout")
            chain_turns("m", 1, Z)
            ready(("m", 1, 1))
            deep(u, 1, AH, AL, 0, True, False, "wout")
            pe.wait_ge(piece_used, 32)
            for c in range(4, 12):
                ada_sum(c, c - 4)
            for tok in range(TOK):
                deep(u + 1, tok, AH, AL, 4, False, True, "wout")
            chain_turns("c1", 0, Z)

            def up_phase(names, blocks, chain, buf, late):
                for i, (unit, key) in enumerate(names):
                    u = UNIT[unit]
                    if i == 0 and chain:
                        ready((chain, 0, 1))
                    wide(u, 0)
                    if i == 0 and chain:
                        chain_turns(chain, 1, buf)
                        ready((chain, 1, 1))
                    for k in late:
                        from_tmp(k, blocks)
                    wide(u, 1)
                    from_tmp(key + (0,), blocks)
                    late = [key + (1,)]
                return late

            def down_phase(names, blocks, late, product, first, last, need):
                for i, (unit, k0) in enumerate(names):
                    u = UNIT[unit]
                    for tok in range(TOK):
                        ready(need[i] + (tok,))
                        deep(u, tok, HH, HL, k0, first and i == 0, last and i == len(names) - 1, product)
                        if tok == 0:
                            for k in late:
                                from_tmp(k, blocks)
                            late = []

            for part in range(2):
                g4 = range(4 * part, 4 * part + 4)
                late = up_phase([(("up", g), ("up", g)) for g in g4], 4, "c1" if part == 0 else None, Z, [])
                down_phase([(("down", g), 4 * (g % 4)) for g in g4], 4, late, "mlp", part == 0, part == 1,
                           [("up", g) for g in g4])
            chain_turns("c2", 0, X)

            def ffn(f, chain):
                late = up_phase([(("gu", f, c), ("gu", f, c)) for c in range(8)], 2, chain, X, [])
                down_phase([(("dn", f, g), 4 * g) for g in range(4)], 2, late, f"f{f}", True, False,
                           [("gu", f, 2 * g + 1) for g in range(4)])
                late = up_phase([(("gu", f, c), ("gu", f, c)) for c in range(8, 11)], 2, None, X, [])
                down_phase([(("dn", f, 4), 0), (("dn", f, 5), 2)], 2, late, f"f{f}", False, True,
                           [("gu", f, 8), ("gu", f, 10)])

            ffn(0, "c2")
            chain_turns(("f", 0), 0, X)
            late = []
            att = 2 * NF
            for i, c in enumerate((0, 2, 4, 1, 3, 5)):
                u = UNIT[("moba", c)]
                if i == 0:
                    ready((("f", 0), 0, 1))
                wide(u, 0)
                if i == 0:
                    chain_turns(("f", 0), 1, X)
                    pe.wait_ge(in_c, 80)
                    rev_row(1)
                    ready((("f", 0), 1, 1))
                for k in late:
                    from_tmp(k, 4)
                late = []
                if i >= 3:
                    slot(att, 2 * NF, 2 * NF + MH)
                    att += 1
                wide(u, 1)
                if c < 4:
                    from_tmp(("moba", c, 0), 4)
                    late = [("moba", c, 1)]
                if i >= 3 and att < 2 * NF + 4:
                    slot(att, 2 * NF, 2 * NF + MH)
                    att += 1
            while att <= 2 * NF + MH:
                slot(att, 2 * NF, 2 * NF + MH)
                att += 1
            pe.wait_ge(y_done, 2 * NF + MH)
            for tok in range(TOK):
                chain_turns("my", tok, YM)
            for g in range(2):
                for tok in range(TOK):
                    ready(("my", tok, g))
                    deep(UNIT[("aout", g)], tok, AH, AL, 4 * g, g == 0, g == 1, "aout")
            chain_turns("c3", 0, X)
            ffn(1, "c3")
            chain_turns(("f", 1), 0, X)
            ffn(2, ("f", 1))
            chain_turns(("f", 2), 0, X)
            for g in range(2):
                u = UNIT[("bin", g)]
                if g == 0:
                    ready((("f", 2), 0, 1))
                deep(u, 0, AH, AL, 4 * g, g == 0, g == 1, "bin")
                if g == 0:
                    chain_turns(("f", 2), 1, X)
                    ready((("f", 2), 1, 1))
                deep(u, 1, AH, AL, 4 * g, g == 0, g == 1, "bin")
            pe.wait_ge(uu_done, 2)
            pe.wait_ge(in_pool, 32)
            for j in range(4):
                dst = bank_of(("pool", j))
                for i in range(2):
                    cb = 2 * j + i
                    for s in range(2):
                        mm = pe.matmul(dst[:, 256 * i:256 * i + 256], UU[:, s, cb * P:(cb + 1) * P],
                                       POOLM[:, cb // 2, s, :], start=(s == 0), stop=(s == 1))
                mm.then_inc(tr_done, 1)
            u = UNIT[("grp",)]
            for tok in range(TOK):
                ts = slice(tok * P, (tok + 1) * P)
                for g in range(4):
                    ready(("pool", g))
                    for k in range(2):
                        o = g * 512 + k * 256
                        quarters(u, tok, o + 256)
                        w = slice(o, o + 256)
                        mm = three(Y[tok][g // 2][:, (g % 2) * 256:(g % 2 + 1) * 256], HH[:, 2 * g + k, ts],
                                   HL[:, 2 * g + k, ts], WH[:, u % 2, w], WL[:, u % 2, w], k == 0, k == 1)
                mm.then_inc(mm_done, 1)
            chain_turns("g", 0, Z)
            for g in range(2):
                u = UNIT[("bout", g)]
                if g == 0:
                    ready(("g", 0, 1))
                deep(u, 0, AH, AL, 4 * g, g == 0, g == 1, "bout")
                if g == 0:
                    chain_turns("g", 1, Z)
                    ready(("g", 1, 1))
                deep(u, 1, AH, AL, 4 * g, g == 0, g == 1, "bout")
            chain_turns("c4", 0, X)
            ffn(3, "c4")

        @block.scalar
        def _(act):
            seq = [0]

            def step(ins):
                seq[0] += 1
                ins.then_inc(s_seq, 1)
                act.wait_ge(s_seq, seq[0])

            def round_unit(u):
                if u >= len(UNITS):
                    return
                _, _, width, kts = UNITS[u]
                n = width * kts // 4
                if u >= 2:
                    act.wait_ge(mm_done, 2 * (u - 2) + 2)
                for q in range(4):
                    if q % 2 == 0:
                        act.wait_ge(raw_in[q // 2], 32 * (u + 1))
                    act.copy(WH[:, u % 2, q * n:(q + 1) * n], RAW[:, q // 2, (q % 2) * n:(q % 2 + 1) * n]
                             ).then_inc(wh_done, 1)

            def high(key, dst, n):
                act.wait_ge(tr_done, TURN[key] + 1)
                act.copy(dst, TB[TURN[key] % 2][:, 0:n].rearrange("p (k n) -> p k n", n=dst.shape[2])
                         ).then_inc(th_done, 1)

            def chain_high(name, tok):
                for h in range(2):
                    high((name, tok, h), AH[:, 4 * h:4 * h + 4, tok * P:(tok + 1) * P], HALF)

            def to_tmp(key, u, tok, n):
                act.wait_ge(mm_done, 2 * u + tok + 1)
                b = TURN[key]
                act.wait_ge(tr_done, b - 1)
                act.copy(TMP[:, b % 2, 0:n], UP[tok][:, 0:n])

            def taken(key, dst, n):
                act.wait_ge(tr_done, TURN[key] + 1)
                act.copy(dst, TB[TURN[key] % 2][:, 0:n].rearrange("p (k n) -> p k n", n=P)
                         ).then_inc(tr_free[TURN[key] % 2], 1)

            def index_in(tok):
                key = ("qi", tok)
                ts = slice(tok * P, (tok + 1) * P)
                act.wait_ge(tr_done, TURN[key] + 1)
                act.copy(QI[:, :, ts], TB[TURN[key] % 2][:, 0:2 * P].rearrange("p (a n) -> p a n", a=2))
                act.copy(KI[:, ts], TB[TURN[key] % 2][:, 2 * P:3 * P]).then_inc(tr_free[TURN[key] % 2], 1)

            def probs(a):
                act.wait_ge(m_done, a + 1)
                z = SB[a % 2] if ITEMS[a][0] == "f" else PR[:, a % 2, :]
                if a >= 2:
                    act.wait_ge(pt_tr, a - 1)
                for tok, lo, hi in ((0, 0, P), (1, P, REV)):
                    ins = act.activation(PR[:, a % 2, lo:hi], z[:, lo:hi], ACT.Exp,
                                         bias=NM[:, a % 2, tok:tok + 1], accum_out=SM[:, a % 2, tok:tok + 1])
                ins.then_inc(p_done, 1)

            def probs_copy(a):
                act.wait_ge(pt_tr, a + 1)
                if a >= 2:
                    act.wait_ge(pv_done, a - 1)
                act.copy(PT[:, a % 2, :], PTB[:, 0:REV]).then_inc(pt_cp, 1)

            def outputs(a):
                _, _, _, y, dh = item_views(a)
                act.wait_ge(rc_done, a + 1)
                act.wait_ge(pv_done, a + 1)
                act.activation(y[:, 0, :], OB[:, 0:dh], ACT.Copy, scale=RC[:, a % 2, 0:1])
                act.activation(y[:, 1, :], OB[:, P:P + dh], ACT.Copy, scale=RC[:, a % 2, 1:2]
                               ).then_inc(y_done, 1)

            def slot(a, first, end):
                if first < a <= end:
                    probs_copy(a - 1)
                if a < end:
                    probs(a)
                if first < a <= end:
                    outputs(a - 1)

            round_unit(0)
            chain_high("h", 0)
            att = 0
            places = {"qd": QD, "kd": KD, "qf": QF, "kf": KF}
            for u in range(11):
                name = UNITS[u][0]
                for tok in range(TOK):
                    if tok == 0:
                        if u == 0:
                            chain_high("h", 1)
                        round_unit(u + 1)
                    before = UNITS[u - 1][0][0] if u else None
                    if u == 1 and tok == 1:
                        taken(("qd", 0), QD[:, :, 0:P], HALF)
                        act.wait_ge(idx_done, 1)
                        for h in range(NI):
                            if h >= 1:
                                act.wait_ge(r_used, h)
                            act.activation(PR[:, 0, :], IDX[h][:, 0:REV], ACT.Relu, scale=DH ** -0.5
                                           ).then_inc(r_done, 1)
                    if u == 0:
                        act.wait_ge(mm_done, tok + 1)
                        b = TURN[("qi", tok)]
                        act.wait_ge(tr_done, b - 1)
                        act.copy(TMP[:, b % 2, 0:320], UP[tok][:, 0:320])
                        act.copy(TMP[:, b % 2, 320:384], UP[tok][:, 256:320]).then_inc(tmp_s, 1)
                        act.wait_ge(lf_in, tok + 1)
                        step(act.activation(LF[:, tok, 1, :], LF[:, tok, 0, :], ACT.Abs))
                        step(act.activation(LF[:, tok, 1, :], LF[:, tok, 1, :], ACT.Exp, scale=-1.0))
                        act.activation(LF[:, tok, 2, :], LF[:, tok, 1, :], ACT.Ln, bias=1.0).then_inc(lf_mid, 1)
                    elif name[0] in places:
                        act.wait_ge(mm_done, 2 * u + tok + 1)
                        b = TURN[(name[0], tok)]
                        act.wait_ge(tr_done, b - 1)
                        act.activation(TMP[:, b % 2, :], UP[tok][:, :], ACT.Copy,
                                       scale=DH ** -0.5 if name[0] == "qf" else 1.0).then_inc(tmp_s, 1)
                    elif name[0] in ("vd", "vf"):
                        act.wait_ge(mm_done, 2 * u + tok + 1)
                        act.copy((VD if name[0] == "vd" else VF)[:, tok, :], UP[tok][:, :]
                                 ).then_inc(up_copied, 1)
                    else:
                        act.wait_ge(mm_done, 2 * u + tok + 1)
                        act.copy(SIG[:, tok, name[1] * HALF:(name[1] + 1) * HALF], UP[tok][:, :]
                                 ).then_inc(up_copied, 1)
                    if tok == 0 and before == "misc":
                        index_in(1)
                    elif tok == 0 and before in places:
                        taken((before, 1), places[before][:, :, P:256], HALF)
                    elif tok == 1 and u == 0:
                        index_in(0)
                    elif tok == 1 and u >= 2 and name[0] in places:
                        taken((name[0], 0), places[name[0]][:, :, 0:P], HALF)
                    if u >= 4:
                        slot(att, 0, 2 * NF)
                        att += 1
            while att <= 2 * NF:
                slot(att, 0, 2 * NF)
                att += 1
            for tok in range(TOK):
                act.activation(SIG[:, tok, :], SIG[:, tok, :], ACT.Sigmoid).then_inc(sig_done, 1)
            for tok in range(TOK):
                chain_high("y", tok)
            round_unit(UNIT[("br", 0)] + 1)
            round_unit(UNIT[("br", 1)] + 1)
            chain_high("m", 0)
            chain_high("m", 1)
            round_unit(UNIT[("wout", 0)] + 1)
            round_unit(UNIT[("wout", 1)] + 1)
            chain_high("c1", 0)

            def up_phase(names, nblk, func, chain, late):
                for i, (unit, key) in enumerate(names):
                    u = UNIT[unit]
                    if i == 0 and chain:
                        chain_high(chain, 1)
                    round_unit(u + 1)
                    for tok in range(TOK):
                        act.wait_ge(mm_done, 2 * u + tok + 1)
                        n = P * nblk
                        if TG_READ[key + (tok,)]:
                            act.wait_ge(tmp_v, TG_READ[key + (tok,)])
                        act.activation(TG[:, tok, 0:n], UP[tok][:, 0:n], func).then_inc(tg_done, 1)
                        if tok == 0:
                            for k, dst in late:
                                high(k, dst, n)
                            late = []
                        else:
                            k0 = key_kt(key)
                            high(key + (0,), HH[:, k0:k0 + nblk, 0:P], n)
                            late = [(key + (1,), HH[:, k0:k0 + nblk, P:256])]
                return late

            def down_phase(units, late, n):
                for i, unit in enumerate(units):
                    round_unit(UNIT[unit] + 1)
                    if i == 0:
                        for k, dst in late:
                            high(k, dst, n)

            for part in range(2):
                g4 = range(4 * part, 4 * part + 4)
                late = up_phase([(("up", g), ("up", g)) for g in g4], 4, ACT.Relu, "c1" if part == 0 else None, [])
                down_phase([("down", g) for g in g4], late, HALF)
            chain_high("c2", 0)

            def ffn(f, chain):
                late = up_phase([(("gu", f, c), ("gu", f, c)) for c in range(8)], 2, ACT.Silu, chain, [])
                down_phase([("dn", f, g) for g in range(4)], late, GC)
                late = up_phase([(("gu", f, c), ("gu", f, c)) for c in range(8, 11)], 2, ACT.Silu, None, [])
                down_phase([("dn", f, 4), ("dn", f, 5)], late, GC)

            ffn(0, "c2")
            chain_high(("f", 0), 0)
            att = 2 * NF
            late = None
            for i, c in enumerate((0, 2, 4, 1, 3, 5)):
                u = UNIT[("moba", c)]
                if i == 0:
                    chain_high(("f", 0), 1)
                round_unit(u + 1)
                for tok in range(TOK):
                    act.wait_ge(mm_done, 2 * u + tok + 1)
                    if c < 4:
                        b = TURN[("moba", c, tok)]
                        act.wait_ge(tr_done, b - 1)
                        act.copy(TMP[:, b % 2, :], UP[tok][:, :]).then_inc(tmp_s, 1)
                    else:
                        act.copy(VM[:, tok, (c - 4) * HALF:(c - 3) * HALF], UP[tok][:, :]
                                 ).then_inc(up_copied, 1)
                    if tok == 0 and late:
                        taken(*late)
                        late = None
                    elif tok == 1 and c < 4:
                        dst = (QM if c < 2 else KM)[:, 4 * (c % 2):4 * (c % 2) + 4, :]
                        taken(("moba", c, 0), dst[:, :, 0:P], HALF)
                        late = (("moba", c, 1), dst[:, :, P:256], HALF)
                    if i >= 3 and (tok == 0 or att < 2 * NF + 4):
                        slot(att, 2 * NF, 2 * NF + MH)
                        att += 1
            while att <= 2 * NF + MH:
                slot(att, 2 * NF, 2 * NF + MH)
                att += 1
            for tok in range(TOK):
                chain_high("my", tok)
            round_unit(UNIT[("aout", 0)] + 1)
            round_unit(UNIT[("aout", 1)] + 1)
            chain_high("c3", 0)
            ffn(1, "c3")
            chain_high(("f", 1), 0)
            ffn(2, ("f", 1))
            chain_high(("f", 2), 0)
            chain_high(("f", 2), 1)
            round_unit(UNIT[("bin", 0)] + 1)
            round_unit(UNIT[("bin", 1)] + 1)
            for tok in range(TOK):
                act.wait_ge(mm_done, 2 * UNIT[("bin", 1)] + tok + 1)
                act.copy(UU[:, tok, 0:HALF], Y[tok][0][:, :])
                act.copy(UU[:, tok, HALF:D], Y[tok][1][:, :]).then_inc(uu_done, 1)
            for j in range(4):
                high(("pool", j), HH[:, 2 * j:2 * j + 2, :], HALF)
            round_unit(UNIT[("grp",)] + 1)
            chain_high("g", 0)
            chain_high("g", 1)
            round_unit(UNIT[("bout", 0)] + 1)
            round_unit(UNIT[("bout", 1)] + 1)
            chain_high("c4", 0)
            ffn(3, "c4")

        @block.vector
        def _(ve):
            seq = [0]

            def step(ins):
                seq[0] += 1
                ins.then_inc(v_seq, 1)
                ve.wait_ge(v_seq, seq[0])

            def split_unit(u):
                if u >= len(UNITS):
                    return
                _, _, width, kts = UNITS[u]
                n = width * kts // 4
                for q in range(4):
                    ve.wait_ge(wh_done, 4 * u + q + 1)
                    o = slice(q * n, (q + 1) * n)
                    ve.tensor_tensor(WL[:, u % 2, o], RAW[:, q // 2, (q % 2) * n:(q % 2 + 1) * n],
                                     WH[:, u % 2, o].bitcast(F32), ALU.subtract).then_inc(wl_done, 1)

            def low(key, dst, hi, n):
                ve.wait_ge(th_done, SPLIT_NO[key])
                ve.tensor_tensor(dst, TB[TURN[key] % 2][:, 0:n].rearrange("p (k n) -> p k n", n=dst.shape[2]),
                                 hi.bitcast(F32), ALU.subtract).then_inc(tr_free[TURN[key] % 2], 1)

            def chain_low(name, tok):
                for h in range(2):
                    s = (slice(None), slice(4 * h, 4 * h + 4), slice(tok * P, (tok + 1) * P))
                    low((name, tok, h), AL[s], AH[s], HALF)

            def plain(key, dst, rows, n):
                ve.wait_ge(tr_done, TURN[key] + 1)
                ve.tensor_copy(dst, TB[TURN[key] % 2][0:rows, 0:n]).then_inc(tr_free[TURN[key] % 2], 1)

            def logits(a):
                kind, h = ITEMS[a]
                z = SB[a % 2]
                ve.wait_ge(s_done, a + 1)
                if kind != "f":
                    scale = P ** -0.5 if kind == "m" else DH ** -0.5
                    z = PR[:, a % 2, :]
                    if a >= 2:
                        ve.wait_ge(pt_tr, a - 1)
                    ve.scalar_tensor_tensor(z[:, 0:P], SB[a % 2][:, 0:P], scale, TAB[:, h, P:TABW],
                                            ALU.mult, ALU.add)
                    step(ve.scalar_tensor_tensor(z[:, P:REV], SB[a % 2][:, P:REV], scale, TAB[:, h, :],
                                                 ALU.mult, ALU.add))
                elif a >= 2:
                    ve.wait_ge(p_done, a - 1)
                ve.tensor_reduce(NM[:, a % 2, 0:1], z[:, 0:P], AX.X, ALU.max, negate=True)
                ve.tensor_reduce(NM[:, a % 2, 1:2], z[:, P:REV], AX.X, ALU.max, negate=True).then_inc(m_done, 1)

            def slot(a, first, end):
                if a < end:
                    logits(a)
                if first < a <= end:
                    ve.wait_ge(p_done, a)
                    ve.reciprocal(RC[:, (a - 1) % 2, :], SM[:, (a - 1) % 2, :]).then_inc(rc_done, 1)

            def stats(buf, tok, rms):
                for h in range(2):
                    ins = ve.bn_stats(ST[:, tok, 6 * h:6 * h + 6], buf[:, tok, h * HALF:(h + 1) * HALF])
                step(ins)
                ins = ve.bn_aggr(MV[:, tok, :], ST[:, tok, :])
                step(ins)
                if rms:
                    ins = ve.scalar_tensor_tensor(VAR[:, tok:tok + 1], MV[:, tok, 0:1], MV[:, tok, 0:1],
                                                  MV[:, tok, 1:2], ALU.mult, ALU.add)
                else:
                    ins = ve.tensor_copy(VAR[:, tok:tok + 1], MV[:, tok, 1:2])
                ins.then_inc(var_done, 1)

            def normalise(name, tok, src, dst, rms, gain, offset, turned=True):
                ve.wait_ge(rs_done, 2 * CHAIN[name] + tok + 1)
                for h in range(2):
                    s = slice(h * HALF, (h + 1) * HALF)
                    if rms:
                        step(ve.tensor_scalar(dst[:, tok, s], src[:, tok, s], RS[:, tok:tok + 1], None, ALU.mult))
                    else:
                        step(ve.tensor_scalar(dst[:, tok, s], src[:, tok, s], MV[:, tok, 0:1],
                                              RS[:, tok:tok + 1], ALU.subtract, ALU.mult))
                    ins = ve.tensor_tensor(dst[:, tok, s], dst[:, tok, s], gain[:, s], ALU.mult)
                    if offset is not None:
                        step(ins)
                        ins = ve.tensor_tensor(dst[:, tok, s], dst[:, tok, s], offset[:, s], ALU.add)
                    if turned:
                        ins.then_inc(tmp_v, 1)
                if not turned:
                    ins.then_inc(out_ready, 1)

            ve.wait_ge(g_seq, CONSTANTS)
            ve.tensor_copy(CMR[:, :], CM[:, :])
            ve.tensor_copy(IDR[:, :], IDENT[:, :]).then_inc(cmr_done, 1)
            ve.wait_ge(in_x, 16)
            for tok in range(TOK):
                stats(X, tok, True)
            ve.wait_ge(in_c, 64)
            ve.wait_ge(g_seq, CONSTANTS)
            ve.wait_ge(in_brow, 16)
            acc = ADA[:, 0:2, :].rearrange("p a n -> p (a n)")
            for k in range(KT):
                ve.wait_ge(in_wada[k % 4], 16 * (k // 4 + 1))
                ins = ve.scalar_tensor_tensor(acc, WADA[:, k % 4, :], CC[:, k:k + 1], acc, ALU.mult, ALU.add)
                ins.then_inc(wada_used, 1)
                ve.wait_ge(wada_used, k + 1)
            plain(("tab", 0), REVROW[:, :], 8, REV)
            split_unit(0)
            for c in range(4):
                plain(("ada", c), ADA[:, c // 2, (c % 2) * HALF:(c % 2 + 1) * HALF], P, HALF)
            ve.wait_ge(in_rows, 16)
            for c in (2, 3):
                ve.wait_ge(*emptied(TURN[("ada", c)]))
            step(ve.scalar_tensor_tensor(ADA[:, 1, :], ADA[:, 1, :], 1.0, ROWS[:, 0, :], ALU.add, ALU.mult))
            normalise("h", 0, X, Z, True, ADA[:, 1, :], ADA[:, 0, :])
            chain_low("h", 0)
            normalise("h", 1, X, Z, True, ADA[:, 1, :], ADA[:, 0, :])
            chain_low("h", 1)

            piece = [0]

            def modulation(n):
                for _ in range(n):
                    i = piece[0]
                    if i >= 32:
                        return
                    if i == 0:
                        ve.wait_ge(in_brow, 32)
                    ve.wait_ge(in_piece[i % 2], 16 * (i // 2 + 1))
                    dst = ADA[:, i // KT, :]
                    ve.scalar_tensor_tensor(dst, PIECE[:, i % 2, :], CC[:, i % KT:i % KT + 1], dst,
                                            ALU.mult, ALU.add).then_inc(piece_used, 1)
                    ve.wait_ge(piece_used, i + 1)
                    piece[0] += 1

            def forget_in(tok):
                ve.wait_ge(tmp_s, tok + 1)
                ve.tensor_scalar(WI[:, tok, :], UP[tok][:, 320:324], NI ** -0.5, None, ALU.mult)
                ve.tensor_tensor(LF[:, tok, 0, :], UP[tok][:, 324:332], BF[:, :], ALU.add).then_inc(lf_in, 1)

            def forget_out(tok):
                ve.wait_ge(lf_mid, tok + 1)
                ve.scalar_tensor_tensor(LFS[:, tok, :], LF[:, tok, 0, :], 0.0, LF[:, tok, 2, :],
                                        ALU.min, ALU.subtract).then_inc(lf_done, 1)

            def top_keys():
                ve.wait_ge(rev_out, 16)
                for h in range(NI):
                    ve.wait_ge(r_done, h + 1)
                    for tok, lo, hi in ((0, 0, P), (1, P, REV)):
                        r, w = PR[:, 0, lo:hi], WI[:, tok, h:h + 1]
                        if h == 0:
                            ins = ve.tensor_scalar(PR[:, 1, lo:hi], r, w, 0.0, ALU.mult, ALU.add)
                        else:
                            ins = ve.scalar_tensor_tensor(PR[:, 1, lo:hi], r, w, PR[:, 1, lo:hi],
                                                          ALU.mult, ALU.add)
                    ins.then_inc(r_used, 1)
                    ve.wait_ge(r_used, h + 1)
                step(ve.tensor_tensor(PR[:, 1, 0:P], PR[:, 1, 0:P], CM[:, P:TABW], ALU.add))
                step(ve.tensor_tensor(PR[:, 1, P:REV], PR[:, 1, P:REV], CM[:, :], ALU.add))
                for lo, hi in ((0, P), (P, REV)):
                    for _ in range(TOPK // 8):
                        step(ve.max(M8[:, :], PR[:, 1, lo:hi]))
                        step(ve.match_replace(PR[:, 1, lo:hi], M8[:, :], PR[:, 1, lo:hi], TAKEN))
                ve.tensor_scalar(SELM[:, :], PR[:, 1, :], TAKEN / 3, MASKED, ALU.is_gt, ALU.mult).then_inc(sel_done, 1)

            att = 0
            for u in range(11):
                split_unit(u + 1)
                if u == 0:
                    forget_in(0)
                    forget_out(0)
                if u >= 4:
                    slot(att, 0, 2 * NF)
                    att += 1
                if u == 0:
                    forget_in(1)
                    forget_out(1)
                if u == 1:
                    ve.wait_ge(tr_done, TURN[("F",)] + 1)
                    ve.tensor_scalar(FT[:, :], TB[TURN[("F",)] % 2][0:NF, 0:256], 1.0, None, ALU.mult)
                    ve.tensor_scalar(FTN[:, :], TB[TURN[("F",)] % 2][0:NF, 0:256], -1.0, None, ALU.mult
                                     ).then_inc(tr_free[TURN[("F",)] % 2], 1)
                    top_keys()
                    ve.wait_ge(in_tab, 16)
                if u >= 4:
                    slot(att, 0, 2 * NF)
                    att += 1
                modulation(2 if u < 4 else 4)
            while att <= 2 * NF:
                slot(att, 0, 2 * NF)
                att += 1
            for tok in range(TOK):
                chain_low("y", tok)
            ve.wait_ge(sig_done, TOK)
            for b in range(2):
                u = UNIT[("br", b)]
                split_unit(u + 1)
                for tok in range(TOK):
                    ve.wait_ge(mm_done, 2 * u + tok + 1)
                    for h in range(2):
                        g = SIG[:, tok, (1 - b) * D + h * HALF:(1 - b) * D + (h + 1) * HALF]
                        z = Z[:, tok, h * HALF:(h + 1) * HALF] if b == 0 else g
                        ins = ve.tensor_tensor(z, Y[tok][h][:, :], g, ALU.mult)
                    ins.then_inc(y_free[tok], 1)
                    ve.wait_ge(y_free[tok], b + 1)
                    for h in range(2 if b == 1 else 0):
                        s = slice(h * HALF, (h + 1) * HALF)
                        ve.tensor_tensor(Z[:, tok, s], Z[:, tok, s], SIG[:, tok, s], ALU.add).then_inc(tmp_v, 1)
                    if b == 1:
                        chain_low("m", tok)
            split_unit(UNIT[("wout", 0)] + 1)
            for c in range(4, 12):
                plain(("ada", c), ADA[:, (c - 4) // 2, (c % 2) * HALF:(c % 2 + 1) * HALF], P, HALF)
            ve.wait_ge(in_rows, 48)
            for c in (10, 11):
                ve.wait_ge(*emptied(TURN[("ada", c)]))
            step(ve.scalar_tensor_tensor(ADA[:, 2, :], ADA[:, 2, :], 1.0, ROWS[:, 0, :], ALU.add, ALU.mult))
            split_unit(UNIT[("wout", 1)] + 1)

            def gated(u, tok, gate):
                ve.wait_ge(mm_done, 2 * u + tok + 1)
                for h in range(2):
                    s = slice(h * HALF, (h + 1) * HALF)
                    ins = ve.tensor_tensor(Z[:, tok, s], Y[tok][h][:, :], gate[:, s], ALU.mult)
                ins.then_inc(y_free[tok], 1)
                ve.wait_ge(y_free[tok], DEEP["wout" if gate is ADA_G1 else "mlp"] + 1)
                step(ve.tensor_tensor(X[:, tok, :], X[:, tok, :], Z[:, tok, :], ALU.add))

            ADA_G1 = ADA[:, 0, :]
            ADA_G2 = ADA[:, 3, :]
            for tok in range(TOK):
                gated(UNIT[("wout", 1)], tok, ADA_G1)
                stats(X, tok, True)
                normalise("c1", tok, X, Z, True, ADA[:, 2, :], ADA[:, 1, :])
                chain_low("c1", tok) if tok == 0 else None

            def up_phase(names, nblk, square, chain, late):
                for i, (unit, key) in enumerate(names):
                    u = UNIT[unit]
                    if i == 0 and chain:
                        chain_low(chain, 1)
                    split_unit(u + 1)
                    n = P * nblk
                    for tok in range(TOK):
                        b = TURN[key + (tok,)]
                        ve.wait_ge(tg_done, TG_NO[key + (tok,)])
                        ve.wait_ge(tr_done, b - 1)
                        other = TG[:, tok, 0:n] if square else UP[tok][:, n:2 * n]
                        ve.tensor_tensor(TMP[:, b % 2, 0:n], TG[:, tok, 0:n], other, ALU.mult).then_inc(tmp_v, 1)
                        if tok == 0:
                            for k, s in late:
                                low(k, HL[s], HH[s], n)
                            late = []
                        else:
                            k0 = key_kt(key)
                            low(key + (0,), HL[:, k0:k0 + nblk, 0:P], HH[:, k0:k0 + nblk, 0:P], n)
                            late = [(key + (1,), (slice(None), slice(k0, k0 + nblk), slice(P, 256)))]
                return late

            def down_phase(units, late, n):
                for i, unit in enumerate(units):
                    split_unit(UNIT[unit] + 1)
                    if i == 0:
                        for k, s in late:
                            low(k, HL[s], HH[s], n)

            for part in range(2):
                g4 = range(4 * part, 4 * part + 4)
                late = up_phase([(("up", g), ("up", g)) for g in g4], 4, True, "c1" if part == 0 else None, [])
                down_phase([("down", g) for g in g4], late, HALF)
            for tok in range(TOK):
                gated(UNIT[("down", 7)], tok, ADA_G2)
                stats(X, tok, True)
                normalise("c2", tok, X, X, True, ROWS[:, 1, :], None)
                chain_low("c2", tok) if tok == 0 else None

            def layer_norm(name, unit, product, factor, rows, turned=True):
                u = UNIT[unit]
                for tok in range(TOK):
                    ve.wait_ge(mm_done, 2 * u + tok + 1)
                    for h in range(2):
                        s = slice(h * HALF, (h + 1) * HALF)
                        ins = ve.scalar_tensor_tensor(Z[:, tok, s], Y[tok][h][:, :], factor, X[:, tok, s],
                                                      ALU.mult, ALU.add)
                    ins.then_inc(y_free[tok], 1)
                    ve.wait_ge(y_free[tok], DEEP[product] + 1)
                    stats(Z, tok, False)
                    ve.wait_ge(in_rows, 48 + 32 * (rows + 1))
                    normalise(name, tok, Z, X, False, ROWS[:, 0, :], ROWS[:, 1, :], turned)
                    if tok == 0 and turned:
                        chain_low(name, tok)
    
            def ffn(f, chain):
                late = up_phase([(("gu", f, c), ("gu", f, c)) for c in range(8)], 2, False, chain, [])
                down_phase([("dn", f, g) for g in range(4)], late, GC)
                late = up_phase([(("gu", f, c), ("gu", f, c)) for c in range(8, 11)], 2, False, None, [])
                down_phase([("dn", f, 4), ("dn", f, 5)], late, GC)

            ffn(0, "c2")
            layer_norm(("f", 0), ("dn", 0, 5), "f0", 0.5 / ALPHA, 0)
            att = 2 * NF
            for i, c in enumerate((0, 2, 4, 1, 3, 5)):
                if i == 0:
                    chain_low(("f", 0), 1)
                    plain(("tab", 1), REVROW[:, :], 8, REV)
                split_unit(UNIT[("moba", c)] + 1)
                for tok in range(TOK):
                    if i >= 3 and (tok == 0 or att < 2 * NF + 4):
                        if att == 2 * NF:
                            ve.wait_ge(in_tab, 32)
                        slot(att, 2 * NF, 2 * NF + MH)
                        att += 1
            while att <= 2 * NF + MH:
                slot(att, 2 * NF, 2 * NF + MH)
                att += 1
            for tok in range(TOK):
                chain_low("my", tok)
            split_unit(UNIT[("aout", 0)] + 1)
            split_unit(UNIT[("aout", 1)] + 1)
            layer_norm("c3", ("aout", 1), "aout", 1 / ALPHA, 1)
            ffn(1, "c3")
            layer_norm(("f", 1), ("dn", 1, 5), "f1", 0.5 / ALPHA, 2)
            ffn(2, ("f", 1))
            layer_norm(("f", 2), ("dn", 2, 5), "f2", 0.5 / ALPHA, 3)
            chain_low(("f", 2), 1)
            split_unit(UNIT[("bin", 0)] + 1)
            split_unit(UNIT[("bin", 1)] + 1)
            for j in range(4):
                low(("pool", j), HL[:, 2 * j:2 * j + 2, :], HH[:, 2 * j:2 * j + 2, :], HALF)
            split_unit(UNIT[("grp",)] + 1)
            for tok in range(TOK):
                ve.wait_ge(mm_done, 2 * UNIT[("grp",)] + tok + 1)
                for h in range(2):
                    s = slice(h * HALF, (h + 1) * HALF)
                    ins = ve.tensor_tensor(Z[:, tok, s], Y[tok][h][:, :], ADA[:, 0, s], ALU.mult)
                    ins.then_inc(tmp_v, 1)
                chain_low("g", tok)
            split_unit(UNIT[("bout", 0)] + 1)
            split_unit(UNIT[("bout", 1)] + 1)
            layer_norm("c4", ("bout", 1), "bout", 1 / ALPHA, 4)
            ffn(3, "c4")
            layer_norm(("f", 3), ("dn", 3, 5), "f3", 0.5 / ALPHA, 5, turned=False)


_INS = ["x", "c", "w_ada", "b_ada", "g_norm1", "w_in", "b_forget", "rel_bias", "w_branch_fox", "w_branch_dsa",
        "w_out", "g_norm2", "w_mlp1", "w_mlp2", "g_final", "rel_bias_2", "ln_g_2", "ln_b_2", "ffn_w_gu_2",
        "ffn_w_down_2", "a_w_in_2", "a_w_out_2", "b_w_in_2", "b_w_group_2", "b_scale_2", "b_w_out_2"]


def reversed_buckets():
    x = np.arange(REV)
    dist = 2 * P - 1 - x
    n = np.maximum(dist, 0)
    exact = NB // 2
    big = exact + (np.log(np.maximum(n, 1).astype(np.float32) / np.float32(exact))
                   / np.float32(np.log(128 / exact)) * np.float32(NB - exact)).astype(np.int32)
    bucket = np.where(n < exact, n, np.minimum(big, NB - 1))
    hot = np.zeros((NB + 1, REV), np.float32)
    hot[np.where(dist >= 0, bucket, NB), x] = 1.0
    return hot


def pooling():
    m = np.zeros((P, len(WINDOWS), TOK, TOK * P), np.float32)
    for g, w in enumerate(WINDOWS):
        for tt in range(TOK * P):
            for s in range(max(0, tt - w + 1), tt + 1):
                m[s % P, g, s // P, tt] += np.float32(1.0 / min(tt + 1, w))
            m[tt % P, g, tt // P, tt] -= 1.0
    return m


def kernel(**inputs):
    import concourse.bacc as _bacc
    from concourse.bass_utils import run_bass_kernel_spmd as _run

    nc = _bacc.Bacc("TRN2", target_bir_lowering=False, num_devices=1)
    arrays, tensors = {}, {}
    given = {name: inputs[name] for name in _INS}
    given["onehot"] = reversed_buckets()
    given["pool_m"] = pooling()
    for name, a in given.items():
        a = np.ascontiguousarray(a)
        arrays[f"in_{name}"] = a
        tensors[name] = nc.dram_tensor(f"in_{name}", a.shape, mybir.dt.from_np(a.dtype), kind="ExternalInput").ap()
    out = nc.dram_tensor("out_0", (1, TOK * P, D), F32, kind="ExternalOutput").ap()
    build(nc, tensors, out)
    r = _run(nc, [arrays], core_ids=[0])
    return r.results[0]["out_0"]
```

```python
from contextlib import ExitStack

import numpy as np

import concourse.bass as bass
from concourse import mybir

P = 128
TOK = 2
D = 1024
KT = D // P
HALF = 512
F32 = mybir.dt.float32
F32R = mybir.dt.float32r
ALU = mybir.AluOpType
ACT = mybir.ActivationFunctionType
AX = mybir.AxisListType

FOX = 512
DSA = 512
NF = 8
DH = 64
NI = 4
TOPK = 64
D_IN = 3 * FOX + NF + 3 * DSA + NI * DH + DH + NI + 2 * D
OFF_F = 3 * FOX
OFF_D = OFF_F + NF
OFF_I = OFF_D + 3 * DSA
N_I = NI * DH + DH + NI
OFF_G = OFF_I + N_I
MISC = N_I + NF
DFF = 4 * D
DFF2 = 2816
GC = 256
NB = 32
MH = 8
ALPHA = 4 ** 0.25
EPS = 1e-6
LN_EPS = 1e-5
MASKED = -1e30
TAKEN = -3e38
WINDOWS = (2, 4, 8, 16)
MODULATION = (2, 0, 1, 0, 3, 3, 3, 3, 3, 3, 3)
PIECES = sum(MODULATION)
CONSTANTS = 8
REV = 384
TABW = 256


def weight_units():
    units = []

    def add(name, kind, width, kts):
        units.append((name, kind, width, kts))

    add(("misc",), "wide", MISC, KT)
    for n in ("qd", "kd", "vd", "qf", "kf", "vf"):
        add((n,), "wide", HALF, KT)
    for g in range(4):
        add(("gate", g), "wide", HALF, KT)
    add(("br", 0), "deep", D, 4)
    add(("br", 1), "deep", D, 4)
    for g in range(2):
        add(("wout", g), "deep", D, 4)
    for part in range(2):
        for g in range(4):
            add(("up", 4 * part + g), "wide", HALF, KT)
        for g in range(4):
            add(("down", 4 * part + g), "deep", D, 4)

    def ffn(f):
        for c in range(8):
            add(("gu", f, c), "wide", HALF, KT)
        for g in range(4):
            add(("dn", f, g), "deep", D, 4)
        for c in range(8, 11):
            add(("gu", f, c), "wide", HALF, KT)
        add(("dn", f, 4), "deep", D, 2)
        add(("dn", f, 5), "deep", D, 4)

    ffn(0)
    for c in (0, 2, 4, 1, 3, 5):
        add(("moba", c), "wide", HALF, KT)
    for g in range(2):
        add(("aout", g), "deep", D, 4)
    ffn(1)
    ffn(2)
    for g in range(2):
        add(("bin", g), "deep", D, 4)
    add(("grp",), "deep", HALF, 4)
    for g in range(2):
        add(("bout", g), "deep", D, 4)
    ffn(3)
    return units


UNITS = weight_units()
UNIT = {u[0]: i for i, u in enumerate(UNITS)}


def psum_turns():
    keys = [("tab", 0)]

    def chain(n):
        keys.extend((n, t, h) for t in range(TOK) for h in range(2))

    chain("h")
    keys.extend([("qi", 0), ("qi", 1), ("qd", 0), ("F",), ("qd", 1), ("kd", 0), ("kd", 1),
                 ("qf", 0), ("qf", 1), ("kf", 0), ("kf", 1)])
    chain("y")
    chain("m")
    keys.extend(("ada", c) for c in range(4, 10))
    chain("c1")
    keys.extend(("up", g, t) for g in range(4) for t in range(TOK))
    keys.extend(("ada", c) for c in (10, 11))
    keys.extend(("up", g, t) for g in range(4, 8) for t in range(TOK))
    chain("c2")

    def ffn(f):
        keys.extend(("gu", f, c, t) for c in range(11) for t in range(TOK))
        chain(("f", f))

    ffn(0)
    keys.append(("tab", 1))
    keys.extend(("moba", c, t) for c in (0, 2, 1, 3) for t in range(TOK))
    chain("my")
    chain("c3")
    ffn(1)
    ffn(2)
    keys.extend(("pool", j) for j in range(4))
    chain("g")
    chain("c4")
    keys.extend(("gu", 3, c, t) for c in range(11) for t in range(TOK))
    return {k: i for i, k in enumerate(keys)}


TURN = psum_turns()
PLAIN = {"tab", "ada", "qi", "qd", "F", "kd", "qf", "kf", "moba"}
BY_SCALAR = {"qi", "qd", "kd", "qf", "kf", "moba"}


def counts(chosen):
    n, out = 0, {}
    for k in TURN:
        if chosen(k):
            n += 1
            out[k] = n
    return out


SPLIT_NO = counts(lambda k: k[0] not in PLAIN)
TMP_S = counts(lambda k: k[0] in BY_SCALAR)
TMP_V = counts(lambda k: k[0] not in BY_SCALAR and k[0] not in ("tab", "ada", "F", "pool", "y", "my"))
TG_NO = counts(lambda k: k[0] in ("up", "gu"))
TG_READ = {}
_last = [0, 0]
for _k in TG_NO:
    TG_READ[_k] = _last[_k[-1]]
    _last[_k[-1]] = TMP_V[_k]


def key_kt(key):
    return 4 * (key[1] % 4) if key[0] == "up" else 2 * (key[2] % 8)


ITEMS = [("d", h) for h in range(NF)] + [("f", h) for h in range(NF)] + [("m", h) for h in range(MH)]
DEEP = {n: i for i, n in enumerate(["br0", "br1", "wout", "mlp", "f0", "aout", "f1", "f2", "bout", "f3"])}
CHAIN = {n: i for i, n in enumerate(["h", "c1", "c2", ("f", 0), "c3", ("f", 1), ("f", 2), "c4", ("f", 3)])}


def build(nc, t, out):
    with ExitStack() as ctx:
        def sb(name, shape, dt=F32):
            return ctx.enter_context(nc.sbuf_tensor(name, shape, dt))

        def bank(name):
            return ctx.enter_context(nc.psum_tensor(name, [P, HALF], F32))

        def sem(name):
            return ctx.enter_context(nc.semaphore(name))

        RAW = sb("RAW", [P, 2, 2048])
        WH = sb("WH", [P, 2, 4096], F32R)
        WL = sb("WL", [P, 2, 4096], F32R)
        AH = sb("AH", [P, KT, 256], F32R)
        AL = sb("AL", [P, KT, 256], F32R)
        hid_at = (nc.sbuf_base + 31) // 32 * 32
        HH = sb("HH", [P, 16, 256], F32R)
        HL = sb("HL", [P, 16, 256], F32R)
        X = sb("X", [P, TOK, D])
        Z = sb("Z", [P, TOK, D])
        ROWS = sb("ROWS", [P, 2, D])
        TAB = sb("TAB", [P, 8, TABW])
        ADA = sb("ADA", [P, 4, D])
        PIECE = sb("PIECE", [P, 2, D])
        TMP = sb("TMP", [P, 2, HALF])
        TG = sb("TG", [P, TOK, HALF])
        PR = sb("PR", [P, 2, REV])
        PT = sb("PT", [P, 2, REV])
        SELM = sb("SELM", [P, REV], F32R)
        CMR = sb("CMR", [P, TABW], F32R)
        IDR = sb("IDR", [P, P], F32R)
        IDENT = sb("IDENT", [P, P])
        TRI = sb("TRI", [P, P])
        ONES = sb("ONES", [P, P])
        CM = sb("CM", [P, TABW])
        FT = sb("FT", [NF, 256])
        FTN = sb("FTN", [NF, 256])
        REL = sb("REL", [64, 8])
        CC = sb("CC", [P, KT])
        BF = sb("BF", [P, NF])
        WI = sb("WI", [P, TOK, NI])
        LF = sb("LF", [P, TOK, 3, NF])
        LFS = sb("LFS", [P, TOK, NF])
        M8 = sb("M8", [P, 8])
        ST = sb("ST", [P, TOK, 12])
        MV = sb("MV", [P, TOK, 2])
        VAR = sb("VAR", [P, TOK])
        RS = sb("RS", [P, TOK])
        SUMS = sb("SUMS", [P, TOK, 2])
        SQ = sb("SQ", [P, TOK, 2])
        MEAN = sb("MEAN", [P, TOK, 2])
        NHALF = sb("NHALF", [P, 1])
        NM = sb("NM", [P, 2, 2])
        SM = sb("SM", [P, 2, 2])
        RC = sb("RC", [P, 2, 2])
        ONEHOT = sb("ONEHOT", [NB + 1, REV])

        def over(name, shape, at):
            return nc.alloc_sbuf_tensor_at(name, shape, F32, offset=hid_at + at)

        WADA = over("WADA", [P, 4, 2 * D], 0)
        QD, KD, QF, KF = (over(n, [P, 4, 256], 4096 * i) for i, n in enumerate(("QD", "KD", "QF", "KF")))
        SIG = over("SIG", [P, TOK, 2 * D], 16384)
        QM = over("QM", [P, MH, 256], 0)
        KM = over("KM", [P, MH, 256], 8192)
        VM = over("VM", [P, TOK, D], 16384)
        YM = over("YM", [P, TOK, D], 24576)
        UU = over("UU", [P, TOK, D], 8192)
        POOLM = over("POOLM", [P, 4, TOK, 256], 24576)
        QI = PT[:, :, :].rearrange("p a b -> p (a b)")[:, 0:512].rearrange("p (a b) -> p a b", a=2)
        KI = PT[:, 1, 128:384]
        REVROW = PR[0:8, 1, :]
        VD = Z[:, :, 0:512]
        VF = Z[:, :, 512:1024]
        YA = ROWS
        REVD = nc.dram_tensor("rev_rows", [2, P, 8, REV], F32, kind="Internal").ap()

        UP = [bank(f"UP{i}") for i in range(TOK)]
        Y = [[bank(f"Y{i}{h}") for h in range(2)] for i in range(TOK)]
        TB = [bank(f"TB{i}") for i in range(2)]
        SB = Y[0]
        PTB = Y[1][0]
        OB = Y[1][1]
        IDX = [Y[0][0], Y[0][1], Y[1][0], Y[1][1]]

        raw_in = [sem("raw_in0"), sem("raw_in1")]
        wh_done = sem("wh_done")
        wl_done = sem("wl_done")
        mm_done = sem("mm_done")
        up_copied = sem("up_copied")
        y_free = [sem("y_free0"), sem("y_free1")]
        tmp_s = sem("tmp_s")
        tmp_v = sem("tmp_v")
        tr_done = sem("tr_done")
        th_done = sem("th_done")
        tr_free = [sem("tr_free0"), sem("tr_free1")]
        tg_done = sem("tg_done")
        s_done = sem("s_done")
        m_done = sem("m_done")
        p_done = sem("p_done")
        pt_tr = sem("pt_tr")
        pt_cp = sem("pt_cp")
        pv_done = sem("pv_done")
        y_done = sem("y_done")
        rc_done = sem("rc_done")
        idx_done = sem("idx_done")
        r_done = sem("r_done")
        r_used = sem("r_used")
        cmr_done = sem("cmr_done")
        sel_done = sem("sel_done")
        lf_in = sem("lf_in")
        lf_mid = sem("lf_mid")
        lf_done = sem("lf_done")
        sig_done = sem("sig_done")
        var_done = sem("var_done")
        sums_done = sem("sums_done")
        sq_done = sem("sq_done")
        rs_done = sem("rs_done")
        v_seq = sem("v_seq")
        s_seq = sem("s_seq")
        g_seq = sem("g_seq")
        in_x = sem("in_x")
        in_c = sem("in_c")
        in_small = sem("in_small")
        ada_done = sem("ada_done")
        in_wada = [sem(f"in_wada{i}") for i in range(4)]
        wada_used = sem("wada_used")
        in_piece = [sem("in_piece0"), sem("in_piece1")]
        piece_used = sem("piece_used")
        in_brow = sem("in_brow")
        in_bias = sem("in_bias")
        in_rows = sem("in_rows")
        rev_out = sem("rev_out")
        in_tab = sem("in_tab")
        uu_done = sem("uu_done")
        in_pool = sem("in_pool")
        out_ready = sem("out_ready")
        out_done = sem("out_done")

        block = ctx.enter_context(nc.Block())

        def taps(u, tile_end):
            _, _, width, kts = UNITS[u]
            quarter = width * kts // 4
            return 4 * u + (tile_end + quarter - 1) // quarter

        up_read = {}
        copies = 0
        for u, (name, kind, _, _) in enumerate(UNITS):
            for tok in range(TOK if kind == "wide" else 0):
                k = name[0]
                if k == "misc":
                    up_read[u, tok] = (lf_done, tok + 1)
                elif k in ("vd", "vf", "gate") or (k == "moba" and name[1] >= 4):
                    copies += 1
                    up_read[u, tok] = (up_copied, copies)
                elif k in BY_SCALAR:
                    up_read[u, tok] = (tmp_s, TMP_S[name + (tok,)])
                elif k == "up":
                    up_read[u, tok] = (tg_done, TG_NO[name + (tok,)])
                else:
                    up_read[u, tok] = (tmp_v, TMP_V[name + (tok,)])
        wides = [u for u, unit in enumerate(UNITS) if unit[1] == "wide"]
        wide_before = dict(zip(wides[1:], wides))

        def emptied(b):
            return tr_free[b % 2], b // 2 + 1

        def item_views(a):
            kind, h = ITEMS[a]
            if kind == "m":
                return (QM[:, h, :], KM[:, h, :], VM[:, :, h * P:(h + 1) * P], YM[:, :, h * P:(h + 1) * P], P)
            q, k, v = (QD, KD, VD) if kind == "d" else (QF, KF, VF)
            o = 0 if kind == "d" else 512
            rows = slice(64 * (h % 2), 64 * (h % 2) + 64)
            return (q[rows, h // 2, :], k[rows, h // 2, :], v[:, :, h * DH:(h + 1) * DH],
                    YA[:, :, o + h * DH:o + (h + 1) * DH], DH)

        @block.sync
        def _(sp):
            gu, dn = t["ffn_w_gu_2"], t["ffn_w_down_2"]

            def src(name):
                k = name[0]
                i, j = (name[1] // 2, name[1] % 2) if k in ("gu", "dn") else (0, 0)
                return {
                    "qd": lambda: (t["w_in"], OFF_D), "kd": lambda: (t["w_in"], OFF_D + DSA),
                    "vd": lambda: (t["w_in"], OFF_D + 2 * DSA), "qf": lambda: (t["w_in"], 0),
                    "kf": lambda: (t["w_in"], FOX), "vf": lambda: (t["w_in"], 2 * FOX),
                    "gate": lambda: (t["w_in"], OFF_G + name[1] * HALF),
                    "br": lambda: ((t["w_branch_dsa"], t["w_branch_fox"])[name[1]], 0),
                    "wout": lambda: (t["w_out"], 0), "up": lambda: (t["w_mlp1"], name[1] * HALF),
                    "down": lambda: (t["w_mlp2"], 0), "gu": lambda: (gu[i, j], name[2] * GC),
                    "dn": lambda: (dn[i, j], 0), "moba": lambda: (t["a_w_in_2"][0], name[1] * HALF),
                    "aout": lambda: (t["a_w_out_2"][0], 0), "bin": lambda: (t["b_w_in_2"][0], 0),
                    "bout": lambda: (t["b_w_out_2"][0], 0),
                }[k]()

            sp.dma_start(CC[:, :], t["c"][0].rearrange("(p k) -> p k", k=KT)).then_inc(in_c, 16)
            sp.dma_start(PIECE[0:1, :, :], t["b_ada"][0:2 * D].rearrange("(o a n) -> o a n", o=1, a=2)
                         ).then_inc(in_brow, 16)
            wada = t["w_ada"].rearrange("(p k) n -> p k n", k=KT)
            for k in range(4):
                sp.dma_start(WADA[:, k, :], wada[:, k, 0:2 * D]).then_inc(in_wada[k], 16)
            sp.dma_start(X[:, :, :], t["x"][0].rearrange("(a p) n -> p a n", p=P)).then_inc(in_x, 16)
            for k in range(4, KT):
                sp.wait_ge(wada_used, k - 3)
                sp.dma_start(WADA[:, k % 4, :], wada[:, k, 0:2 * D]).then_inc(in_wada[k % 4], 16)

            for u, (name, kind, width, kts) in enumerate(UNITS):
                for half in range(2):
                    if u:
                        sp.wait_ge(wl_done, 4 * u - 2 + 2 * half)
                    n = width * kts // 2
                    dst = RAW[:, half, 0:n]
                    if name[0] == "misc":
                        w = t["w_in"].rearrange("(k p) n -> p k n", p=P)[:, 4 * half:4 * half + 4, :]
                        d = dst.rearrange("p (k n) -> p k n", k=4)
                        parts = [(d[:, :, 0:N_I], w[:, :, OFF_I:OFF_I + N_I]),
                                 (d[:, :, N_I:MISC], w[:, :, OFF_F:OFF_F + NF])]
                    elif name[0] == "grp":
                        w = t["b_w_group_2"][0]
                        parts = [(dst[:, 512 * g:512 * g + 512].rearrange("p (k n) -> p k n", k=2),
                                  w[2 * half + g].rearrange("(k p) n -> p k n", p=P)) for g in range(2)]
                    elif name[0] == "gu":
                        m, c = src(name)
                        w = m.rearrange("(k p) n -> p k n", p=P)[:, 4 * half:4 * half + 4, :]
                        d = dst.rearrange("p (k g n) -> p k g n", k=4, g=2)
                        parts = [(d[:, :, g, :], w[:, :, g * DFF2 + c:g * DFF2 + c + GC]) for g in range(2)]
                    elif kind == "wide":
                        m, c = src(name)
                        w = m.rearrange("(k p) n -> p k n", p=P)
                        d = dst.rearrange("p (k n) -> p k n", k=4)
                        parts = [(d[:, 2 * g:2 * g + 2, :],
                                  w[:, 4 * half + 2 * g:4 * half + 2 * g + 2, c:c + HALF]) for g in range(2)]
                    else:
                        m, _ = src(name)
                        k0 = {("dn", 5): 18}.get((name[0], name[-1]), 0 if name[0] == "br" else 4 * name[-1])
                        k0 += (kts // 2) * half
                        w = m.rearrange("(k p) n -> p k n", p=P)
                        d = dst.rearrange("p (k n) -> p k n", n=D)
                        if kts == 4:
                            parts = [(d[:, g, :], w[:, k0 + g, :]) for g in range(2)]
                        else:
                            parts = [(d[:, 0, 512 * g:512 * g + 512], w[:, k0, 512 * g:512 * g + 512])
                                     for g in range(2)]
                    for dd, ss in parts:
                        sp.dma_start(dd, ss).then_inc(raw_in[half], 16)
            for tok in range(TOK):
                for h in range(2):
                    s = slice(h * HALF, (h + 1) * HALF)
                    sp.wait_ge(out_ready, 2 * tok + h + 1)
                    sp.dma_start(out[0, tok * P:(tok + 1) * P, s], X[:, tok, s]).then_inc(out_done, 16)
            sp.wait_ge(out_done, 32 * TOK)

        @block.gpsimd
        def _(gp):
            seq = [0]

            def step(ins):
                seq[0] += 1
                ins.then_inc(g_seq, 1)
                gp.wait_ge(g_seq, seq[0])

            gp.dma_start(BF[:, :], t["b_forget"].partition_broadcast(P)).then_inc(in_small, 16)
            gp.dma_start(REL[0:NB, :], t["rel_bias"]).then_inc(in_small, 16)
            gp.dma_start(ONEHOT[:, :], t["onehot"]).then_inc(in_small, 16)
            gp.dma_start(ROWS[:, 0, :], t["g_norm1"].partition_broadcast(P)).then_inc(in_rows, 16)
            step(gp.memset(REL[NB:NB + 1, :], MASKED))
            step(gp.memset(NHALF[:, :], -0.5))
            step(gp.memset(ONES[:, :], 1.0))
            step(gp.memset(IDENT[:, :], 0.0))
            step(gp.affine_select(out=IDENT[:, :], in_=IDENT[:, :], compare_op=ALU.not_equal, fill=1.0, base=0,
                                  pattern=[[-1, P]], channel_multiplier=1))
            step(gp.affine_select(out=TRI[:, :], in_=ONES[:, :], compare_op=ALU.is_ge, fill=0.0, base=0,
                                  pattern=[[1, P]], channel_multiplier=-1))
            step(gp.memset(CM[:, :], 0.0))
            step(gp.affine_select(out=CM[:, :], in_=CM[:, :], compare_op=ALU.is_ge, fill=MASKED, base=P,
                                  pattern=[[-1, TABW]], channel_multiplier=1))
            assert seq[0] == CONSTANTS

            def table(n):
                gp.wait_ge(*emptied(TURN[("tab", n)]))
                gp.dma_start(REVD[n].rearrange("c h x -> h c x"),
                             REVROW[:, :].unsqueeze(1).to_broadcast([8, P, REV])).then_inc(rev_out, 16)
                gp.wait_ge(rev_out, 16 * (n + 1))
                start = REVD[n, 0, 0, P - 1:P]
                gp.dma_start(TAB[:, :, :], bass.AP(start.tensor, start.offset, [[8 * REV - 1, P], [REV, 8], [1, TABW]])
                             ).then_inc(in_tab, 16)

            def rsqrt(n, eps):
                for tok in range(TOK):
                    if n == 0:
                        gp.wait_ge(var_done, tok + 1)
                        a, b = VAR[:, tok:tok + 1], 0.0
                    else:
                        gp.wait_ge(sq_done, 2 * (n - 1) + tok + 1)
                        a, b = SQ[:, tok, 0:1], SQ[:, tok, 1:2]
                    step(gp.tensor_scalar(VAR[:, tok:tok + 1], a, b, eps, ALU.add, ALU.add))
                    gp.tensor_tensor(RS[:, tok:tok + 1], VAR[:, tok:tok + 1], NHALF[:, :], ALU.pow
                                     ).then_inc(rs_done, 1)
                    gp.wait_ge(rs_done, 2 * n + tok + 1)

            rsqrt(0, EPS)
            table(0)
            gp.wait_ge(tmp_v, TMP_V[("h", 1, 1)])
            step(gp.memset(ADA[:, :, :], 0.0))
            gp.dma_start(ADA[0:1, :, :], t["b_ada"][2 * D:6 * D].rearrange("(o a n) -> o a n", o=1, a=4)
                         ).then_inc(in_bias, 16)
            wada = t["w_ada"].rearrange("(p k) n -> p k n", k=KT)

            def pieces(first, end):
                for i in range(first, end):
                    if i >= 2:
                        gp.wait_ge(piece_used, i - 1)
                    gp.dma_start(PIECE[:, i % 2, :], wada[:, i % KT, 2 * D + (i // KT) * D:3 * D + (i // KT) * D]
                                 ).then_inc(in_piece[i % 2], 16)

            pieces(0, PIECES + 2)
            gp.wait_ge(tr_done, TURN[("y", 1, 1)] + 1)
            gp.dma_start(ROWS[:, 0, :], t["g_norm2"].partition_broadcast(P)).then_inc(in_rows, 16)
            gp.dma_start(ROWS[:, 1, :], t["g_final"].partition_broadcast(P)).then_inc(in_rows, 16)
            rsqrt(1, EPS)
            pieces(PIECES + 2, 32)
            rsqrt(2, EPS)

            def rows(before, layer, j):
                gp.wait_ge(tmp_v, TMP_V[(before, 1, 1)])
                gp.dma_start(ROWS[:, 0, :], t["ln_g_2"][layer, j].partition_broadcast(P)).then_inc(in_rows, 16)
                gp.dma_start(ROWS[:, 1, :], t["ln_b_2"][layer, j].partition_broadcast(P)).then_inc(in_rows, 16)

            rows("c2", 0, 0)
            gp.wait_ge(y_done, 2 * NF)
            gp.dma_start(REL[0:NB, :], t["rel_bias_2"]).then_inc(in_small, 16)
            rsqrt(3, LN_EPS / ALPHA ** 2)
            table(1)
            rows(("f", 0), 0, 1)
            rsqrt(4, LN_EPS / ALPHA ** 2)
            rows("c3", 0, 2)
            rsqrt(5, LN_EPS / ALPHA ** 2)
            rows(("f", 1), 1, 0)
            gp.dma_start(ADA[:, 0, :], t["b_scale_2"][0].partition_broadcast(P)).then_inc(in_pool, 16)
            rsqrt(6, LN_EPS / ALPHA ** 2)
            gp.wait_ge(mm_done, 2 * UNIT[("dn", 2, 5)] + 2)
            gp.dma_start(POOLM[:, :, :, :], t["pool_m"]).then_inc(in_pool, 16)
            rows(("f", 2), 1, 1)
            rsqrt(7, LN_EPS / ALPHA ** 2)
            rows("c4", 1, 2)
            rsqrt(8, LN_EPS / ALPHA ** 2)

        @block.tensor
        def _(pe):
            def three(dst, ah, al, wh, wl, first, last):
                pe.matmul(dst, ah, wh, start=first, stop=False)
                pe.matmul(dst, ah, wl, start=False, stop=False)
                return pe.matmul(dst, al, wh, start=False, stop=last)

            def quarters(u, tok, end):
                if tok == 0:
                    pe.wait_ge(wl_done, taps(u, end))

            def wide(u, tok, chain=None):
                _, _, width, kts = UNITS[u]
                if u in wide_before:
                    pe.wait_ge(*up_read[wide_before[u], tok])
                ts = slice(tok * P, (tok + 1) * P)
                for k in range(kts):
                    if chain and k % 4 == 0:
                        ready((chain, tok, k // 4))
                    quarters(u, tok, (k + 1) * width)
                    w = slice(k * width, (k + 1) * width)
                    mm = three(UP[tok][:, 0:width], AH[:, k, ts], AL[:, k, ts], WH[:, u % 2, w], WL[:, u % 2, w],
                               k == 0, k == kts - 1)
                mm.then_inc(mm_done, 1)

            def deep(u, tok, ah, al, k0, first, last, product):
                kts = UNITS[u][3]
                ts = slice(tok * P, (tok + 1) * P)
                if first and DEEP.get(product):
                    pe.wait_ge(y_free[tok], DEEP[product])
                for k in range(kts):
                    for h in range(2):
                        o = k * D + h * HALF
                        quarters(u, tok, o + HALF)
                        w = slice(o, o + HALF)
                        mm = three(Y[tok][h][:, :], ah[:, k0 + k, ts], al[:, k0 + k, ts], WH[:, u % 2, w],
                                   WL[:, u % 2, w], first and k == 0, last and k == kts - 1)
                mm.then_inc(mm_done, 1)

            def bank_of(key):
                b = TURN[key]
                if b >= 2:
                    pe.wait_ge(*emptied(b - 2))
                return TB[b % 2]

            def turn(key, blocks, source):
                dst = bank_of(key)
                if key in TMP_S:
                    pe.wait_ge(tmp_s, TMP_S[key])
                elif key in TMP_V:
                    pe.wait_ge(tmp_v, TMP_V[key])
                for i in range(blocks):
                    mm = pe.transpose(dst[:, i * P:(i + 1) * P], source[:, i * P:(i + 1) * P], IDENT[:, :])
                mm.then_inc(tr_done, 1)

            def from_tmp(key, blocks):
                turn(key, blocks, TMP[:, TURN[key] % 2, :])

            def chain_turns(name, tok, buf):
                for h in range(2):
                    turn((name, tok, h), 4, buf[:, tok, h * HALF:(h + 1) * HALF])

            def ready(key):
                pe.wait_ge(*emptied(TURN[key]))

            def score(a):
                kind, h = ITEMS[a]
                q, k, _, _, _ = item_views(a)
                if h == 0 or (kind, h) == ("m", 4):
                    ready({"d": ("kd", 1), "f": ("kf", 1), "m": ("moba", 2 + h // 4, 1)}[kind])
                if a == 0:
                    pe.wait_ge(sel_done, 2)
                if a >= 2:
                    pe.wait_ge(p_done, a - 1)
                last = kind == "m"
                for lo, hi, ql, n in ((0, P, 0, P), (P, REV, P, 256)):
                    dst = SB[a % 2][:, lo:hi]
                    mm = pe.matmul(dst, q[:, ql:ql + P], k[:, 0:n], start=True, stop=last)
                    if kind == "f":
                        pick = IDENT[0:NF, h:h + 1]
                        pe.matmul(dst, pick.to_broadcast([NF, P]), FTN[:, 0:n], start=False, stop=False)
                        pe.matmul(dst, FT[:, ql:ql + P], pick.to_broadcast([NF, n]), start=False, stop=False)
                    if kind != "m":
                        mask = CMR[:, 256 - n:256] if kind == "f" else SELM[:, lo:hi]
                        mm = pe.matmul(dst, IDR[:, :], mask, start=False, stop=True)
                mm.then_inc(s_done, 1)

            def turn_probs(a):
                pe.wait_ge(p_done, a + 1)
                if a:
                    pe.wait_ge(pt_cp, a)
                for i in range(3):
                    mm = pe.transpose(PTB[:, i * P:(i + 1) * P], PR[:, a % 2, i * P:(i + 1) * P], IDENT[:, :])
                mm.then_inc(pt_tr, 1)

            def values(a):
                _, _, v, _, dh = item_views(a)
                pe.wait_ge(pt_cp, a + 1)
                if a:
                    pe.wait_ge(y_done, a)
                pt = PT[:, a % 2, :]
                pe.matmul(OB[:, 0:dh], pt[:, 0:P], v[:, 0, :], start=True, stop=True)
                pe.matmul(OB[:, P:P + dh], pt[:, P:2 * P], v[:, 0, :], start=True, stop=False)
                pe.matmul(OB[:, P:P + dh], pt[:, 2 * P:3 * P], v[:, 1, :], start=False, stop=True
                          ).then_inc(pv_done, 1)

            def slot(a, first, end):
                if first < a <= end:
                    turn_probs(a - 1)
                if a < end:
                    score(a)
                if first < a <= end:
                    values(a - 1)

            pe.wait_ge(in_small, 48)
            pe.wait_ge(g_seq, CONSTANTS)
            pe.wait_ge(cmr_done, 1)

            def rev_row(n):
                dst = bank_of(("tab", n))
                pe.matmul(dst[0:8, 0:REV], REL[0:NB + 1, :], ONEHOT[:, :], start=True, stop=True
                          ).then_inc(tr_done, 1)

            def ada_sum(c, col):
                dst = bank_of(("ada", c))
                pe.matmul(dst[:, :], ONES[:, :], ADA[:, col // 2, (col % 2) * HALF:(col % 2 + 1) * HALF],
                          start=True, stop=True).then_inc(tr_done, 1)

            rev_row(0)
            parts = [(1, 0), (0, 0), (1, 1), (0, 1)]
            pe.wait_ge(in_brow, 16)
            for row, h in parts:
                pe.matmul(Y[row][h][:, :], ONES[0:1, :], PIECE[0:1, row, h * HALF:(h + 1) * HALF],
                          start=True, stop=False)
            pe.wait_ge(wada_used, KT)
            for row, h in parts:
                pe.matmul(Y[row][h][:, :], ONES[:, :], ADA[:, row, h * HALF:(h + 1) * HALF],
                          start=False, stop=True).then_inc(ada_done, 1)
            chain_turns("h", 0, Z)
            att = 0
            late = []
            for u in range(11):
                name = UNITS[u][0]
                wide(u, 0, "h" if u == 0 else None)
                if u == 0:
                    chain_turns("h", 1, Z)
                for key, n in late:
                    from_tmp(key, n)
                late = []
                if u >= 4:
                    slot(att, 0, 2 * NF)
                    att += 1
                wide(u, 1, "h" if u == 0 else None)
                if name[0] in ("misc", "qd", "kd", "qf", "kf"):
                    key, n = ("qi", 3) if name[0] == "misc" else (name[0], 4)
                    from_tmp((key, 0), n)
                    late = [((key, 1), n)]
                if u == 1:
                    dst = bank_of(("F",))
                    pe.wait_ge(lf_done, 2)
                    pe.matmul(dst[0:NF, 0:P], LFS[:, 0, :], TRI[:, :], start=True, stop=True)
                    pe.matmul(dst[0:NF, P:256], LFS[:, 1, :], TRI[:, :], start=True, stop=False)
                    pe.matmul(dst[0:NF, P:256], LFS[:, 0, :], ONES[:, :], start=False, stop=True
                              ).then_inc(tr_done, 1)
                    ready(("qi", 1))
                    for h in range(NI):
                        r = slice(64 * (h % 2), 64 * (h % 2) + 64)
                        pe.matmul(IDX[h][:, 0:P], QI[r, h // 2, 0:P], KI[r, 0:P], start=True, stop=True)
                        mm = pe.matmul(IDX[h][:, P:REV], QI[r, h // 2, P:256], KI[r, 0:256],
                                       start=True, stop=True)
                    mm.then_inc(idx_done, 1)
                if u >= 4:
                    slot(att, 0, 2 * NF)
                    att += 1
            while att <= 2 * NF:
                slot(att, 0, 2 * NF)
                att += 1
            pe.wait_ge(y_done, 2 * NF)
            for tok in range(TOK):
                chain_turns("y", tok, YA)
            for b in range(2):
                u = UNIT[("br", b)]
                for tok in range(TOK):
                    ready(("y", tok, b))
                    deep(u, tok, AH, AL, 4 * b, True, True, f"br{b}")
            chain_turns("m", 0, Z)

            u = UNIT[("wout", 0)]
            ready(("m", 0, 0))
            deep(u, 0, AH, AL, 0, True, False, "wout")
            chain_turns("m", 1, Z)
            ready(("m", 1, 0))
            deep(u, 1, AH, AL, 0, True, False, "wout")
            pe.wait_ge(piece_used, PIECES)
            for c in range(4, 10):
                ada_sum(c, c - 4)
            for tok in range(TOK):
                ready(("m", tok, 1))
                deep(u + 1, tok, AH, AL, 4, False, True, "wout")
            chain_turns("c1", 0, Z)

            def up_phase(names, blocks, chain, buf, late):
                for i, (unit, key) in enumerate(names):
                    u = UNIT[unit]
                    wide(u, 0, chain)
                    if chain:
                        chain_turns(chain, 1, buf)
                    for k in late:
                        from_tmp(k, blocks)
                    wide(u, 1, chain)
                    chain = None
                    from_tmp(key + (0,), blocks)
                    late = [key + (1,)]
                return late

            def down_phase(names, blocks, late, product, first, last, need):
                for i, (unit, k0) in enumerate(names):
                    u = UNIT[unit]
                    for tok in range(TOK):
                        ready(need[i] + (tok,))
                        deep(u, tok, HH, HL, k0, first and i == 0, last and i == len(names) - 1, product)
                        if tok == 0:
                            for k in late:
                                from_tmp(k, blocks)
                            late = []

            for part in range(2):
                g4 = range(4 * part, 4 * part + 4)
                late = up_phase([(("up", g), ("up", g)) for g in g4], 4, "c1" if part == 0 else None, Z, [])
                down_phase([(("down", g), 4 * (g % 4)) for g in g4], 4, late, "mlp", part == 0, part == 1,
                           [("up", g) for g in g4])
                if part == 0:
                    pe.wait_ge(piece_used, 32)
                    for c in (10, 11):
                        ada_sum(c, c - 4)
            chain_turns("c2", 0, X)

            def ffn(f, chain):
                late = up_phase([(("gu", f, c), ("gu", f, c)) for c in range(8)], 2, chain, X, [])
                down_phase([(("dn", f, g), 4 * g) for g in range(4)], 2, late, f"f{f}", True, False,
                           [("gu", f, 2 * g + 1) for g in range(4)])
                late = up_phase([(("gu", f, c), ("gu", f, c)) for c in range(8, 11)], 2, None, X, [])
                down_phase([(("dn", f, 4), 0), (("dn", f, 5), 2)], 2, late, f"f{f}", False, True,
                           [("gu", f, 8), ("gu", f, 10)])

            ffn(0, "c2")
            chain_turns(("f", 0), 0, X)
            late = []
            att = 2 * NF
            for i, c in enumerate((0, 2, 4, 1, 3, 5)):
                u = UNIT[("moba", c)]
                chain = ("f", 0) if i == 0 else None
                wide(u, 0, chain)
                if i == 0:
                    chain_turns(("f", 0), 1, X)
                    pe.wait_ge(in_small, 64)
                    rev_row(1)
                for k in late:
                    from_tmp(k, 4)
                late = []
                if i >= 3:
                    slot(att, 2 * NF, 2 * NF + MH)
                    att += 1
                wide(u, 1, chain)
                if c < 4:
                    from_tmp(("moba", c, 0), 4)
                    late = [("moba", c, 1)]
                if i >= 3 and att < 2 * NF + 4:
                    slot(att, 2 * NF, 2 * NF + MH)
                    att += 1
            while att <= 2 * NF + MH:
                slot(att, 2 * NF, 2 * NF + MH)
                att += 1
            pe.wait_ge(y_done, 2 * NF + MH)
            for tok in range(TOK):
                chain_turns("my", tok, YM)
            for g in range(2):
                for tok in range(TOK):
                    ready(("my", tok, g))
                    deep(UNIT[("aout", g)], tok, AH, AL, 4 * g, g == 0, g == 1, "aout")
            chain_turns("c3", 0, X)
            ffn(1, "c3")
            chain_turns(("f", 1), 0, X)
            ffn(2, ("f", 1))
            chain_turns(("f", 2), 0, X)
            for g in range(2):
                u = UNIT[("bin", g)]
                ready((("f", 2), 0, g))
                deep(u, 0, AH, AL, 4 * g, g == 0, g == 1, "bin")
                if g == 0:
                    chain_turns(("f", 2), 1, X)
                ready((("f", 2), 1, g))
                deep(u, 1, AH, AL, 4 * g, g == 0, g == 1, "bin")
            pe.wait_ge(uu_done, 2)
            pe.wait_ge(in_pool, 32)
            for j in range(4):
                dst = bank_of(("pool", j))
                for i in range(2):
                    cb = 2 * j + i
                    for s in range(2):
                        mm = pe.matmul(dst[:, 256 * i:256 * i + 256], UU[:, s, cb * P:(cb + 1) * P],
                                       POOLM[:, cb // 2, s, :], start=(s == 0), stop=(s == 1))
                mm.then_inc(tr_done, 1)
            u = UNIT[("grp",)]
            for tok in range(TOK):
                ts = slice(tok * P, (tok + 1) * P)
                for g in range(4):
                    ready(("pool", g))
                    for k in range(2):
                        o = g * 512 + k * 256
                        quarters(u, tok, o + 256)
                        w = slice(o, o + 256)
                        mm = three(Y[tok][g // 2][:, (g % 2) * 256:(g % 2 + 1) * 256], HH[:, 2 * g + k, ts],
                                   HL[:, 2 * g + k, ts], WH[:, u % 2, w], WL[:, u % 2, w], k == 0, k == 1)
                mm.then_inc(mm_done, 1)
            chain_turns("g", 0, Z)
            for g in range(2):
                u = UNIT[("bout", g)]
                ready(("g", 0, g))
                deep(u, 0, AH, AL, 4 * g, g == 0, g == 1, "bout")
                if g == 0:
                    chain_turns("g", 1, Z)
                ready(("g", 1, g))
                deep(u, 1, AH, AL, 4 * g, g == 0, g == 1, "bout")
            chain_turns("c4", 0, X)
            ffn(3, "c4")

        @block.scalar
        def _(act):
            seq = [0]

            def step(ins):
                seq[0] += 1
                ins.then_inc(s_seq, 1)
                act.wait_ge(s_seq, seq[0])

            def round_unit(u, quarters=range(4)):
                if u >= len(UNITS):
                    return
                _, _, width, kts = UNITS[u]
                n = width * kts // 4
                if u >= 2:
                    act.wait_ge(mm_done, 2 * (u - 2) + 2)
                for q in quarters:
                    if q % 2 == 0:
                        act.wait_ge(raw_in[q // 2], 32 * (u + 1))
                    act.copy(WH[:, u % 2, q * n:(q + 1) * n], RAW[:, q // 2, (q % 2) * n:(q % 2 + 1) * n]
                             ).then_inc(wh_done, 1)

            def high(key, dst, n):
                act.wait_ge(tr_done, TURN[key] + 1)
                act.copy(dst, TB[TURN[key] % 2][:, 0:n].rearrange("p (k n) -> p k n", n=dst.shape[2])
                         ).then_inc(th_done, 1)

            def chain_high(name, tok):
                for h in range(2):
                    high((name, tok, h), AH[:, 4 * h:4 * h + 4, tok * P:(tok + 1) * P], HALF)

            def squares(name, tok, rms):
                src, bias = (X, 0.0) if rms else (Z, MEAN[:, tok, 1:2])
                act.wait_ge(sums_done, 2 * CHAIN[name] + tok - 1)
                for h in range(2):
                    ins = act.activation(TG[:, h, :], src[:, tok, h * HALF:(h + 1) * HALF], ACT.Square,
                                         bias=bias, scale=D ** -0.5, accum_out=SQ[:, tok, h:h + 1])
                ins.then_inc(sq_done, 1)

            def norm_high(name, u, rms):
                squares(name, 0, rms)
                round_unit(u, (2, 3))
                chain_high(name, 0)
                squares(name, 1, rms)

            def taken(key, dst, n):
                act.wait_ge(tr_done, TURN[key] + 1)
                act.copy(dst, TB[TURN[key] % 2][:, 0:n].rearrange("p (k n) -> p k n", n=P)
                         ).then_inc(tr_free[TURN[key] % 2], 1)

            def index_in(tok):
                key = ("qi", tok)
                ts = slice(tok * P, (tok + 1) * P)
                act.wait_ge(tr_done, TURN[key] + 1)
                act.copy(QI[:, :, ts], TB[TURN[key] % 2][:, 0:2 * P].rearrange("p (a n) -> p a n", a=2))
                act.copy(KI[:, ts], TB[TURN[key] % 2][:, 2 * P:3 * P]).then_inc(tr_free[TURN[key] % 2], 1)

            def probs(a):
                act.wait_ge(m_done, a + 1)
                z = SB[a % 2] if ITEMS[a][0] == "f" else PR[:, a % 2, :]
                if a >= 2:
                    act.wait_ge(pt_tr, a - 1)
                for tok, lo, hi in ((0, 0, P), (1, P, REV)):
                    ins = act.activation(PR[:, a % 2, lo:hi], z[:, lo:hi], ACT.Exp,
                                         bias=NM[:, a % 2, tok:tok + 1], accum_out=SM[:, a % 2, tok:tok + 1])
                ins.then_inc(p_done, 1)

            def probs_copy(a):
                act.wait_ge(pt_tr, a + 1)
                if a >= 2:
                    act.wait_ge(pv_done, a - 1)
                act.copy(PT[:, a % 2, :], PTB[:, 0:REV]).then_inc(pt_cp, 1)

            def outputs(a):
                _, _, _, y, dh = item_views(a)
                act.wait_ge(rc_done, a + 1)
                act.wait_ge(pv_done, a + 1)
                act.activation(y[:, 0, :], OB[:, 0:dh], ACT.Copy, scale=RC[:, a % 2, 0:1])
                act.activation(y[:, 1, :], OB[:, P:P + dh], ACT.Copy, scale=RC[:, a % 2, 1:2]
                               ).then_inc(y_done, 1)

            def slot(a, first, end):
                if first < a <= end:
                    probs_copy(a - 1)
                if a < end:
                    probs(a)
                if first < a <= end:
                    outputs(a - 1)

            round_unit(0, (0, 1))
            chain_high("h", 0)
            round_unit(0, (2, 3))
            att = 0
            places = {"qd": QD, "kd": KD, "qf": QF, "kf": KF}
            for u in range(11):
                name = UNITS[u][0]
                for tok in range(TOK):
                    if tok == 0:
                        if u == 0:
                            chain_high("h", 1)
                        round_unit(u + 1)
                    before = UNITS[u - 1][0][0] if u else None
                    if u == 1 and tok == 1:
                        taken(("qd", 0), QD[:, :, 0:P], HALF)
                        act.wait_ge(idx_done, 1)
                        for h in range(NI):
                            if h >= 1:
                                act.wait_ge(r_used, h)
                            act.activation(PR[:, 0, :], IDX[h][:, 0:REV], ACT.Relu, scale=DH ** -0.5
                                           ).then_inc(r_done, 1)
                    if u == 0:
                        act.wait_ge(mm_done, tok + 1)
                        b = TURN[("qi", tok)]
                        act.wait_ge(tr_done, b - 1)
                        act.copy(TMP[:, b % 2, 0:320], UP[tok][:, 0:320])
                        act.copy(TMP[:, b % 2, 320:384], UP[tok][:, 256:320]).then_inc(tmp_s, 1)
                        act.wait_ge(lf_in, tok + 1)
                        step(act.activation(LF[:, tok, 1, :], LF[:, tok, 0, :], ACT.Abs))
                        step(act.activation(LF[:, tok, 1, :], LF[:, tok, 1, :], ACT.Exp, scale=-1.0))
                        act.activation(LF[:, tok, 2, :], LF[:, tok, 1, :], ACT.Ln, bias=1.0).then_inc(lf_mid, 1)
                    elif name[0] in places:
                        act.wait_ge(mm_done, 2 * u + tok + 1)
                        b = TURN[(name[0], tok)]
                        act.wait_ge(tr_done, b - 1)
                        act.activation(TMP[:, b % 2, :], UP[tok][:, :], ACT.Copy,
                                       scale=DH ** -0.5 if name[0] == "qf" else 1.0).then_inc(tmp_s, 1)
                    elif name[0] in ("vd", "vf"):
                        act.wait_ge(mm_done, 2 * u + tok + 1)
                        act.copy((VD if name[0] == "vd" else VF)[:, tok, :], UP[tok][:, :]
                                 ).then_inc(up_copied, 1)
                    else:
                        act.wait_ge(mm_done, 2 * u + tok + 1)
                        act.copy(SIG[:, tok, name[1] * HALF:(name[1] + 1) * HALF], UP[tok][:, :]
                                 ).then_inc(up_copied, 1)
                    if tok == 0 and before == "misc":
                        index_in(1)
                    elif tok == 0 and before in places:
                        taken((before, 1), places[before][:, :, P:256], HALF)
                    elif tok == 1 and u == 0:
                        index_in(0)
                    elif tok == 1 and u >= 2 and name[0] in places:
                        taken((name[0], 0), places[name[0]][:, :, 0:P], HALF)
                    if u >= 4:
                        slot(att, 0, 2 * NF)
                        att += 1
            while att <= 2 * NF:
                slot(att, 0, 2 * NF)
                att += 1
            for tok in range(TOK):
                chain_high("y", tok)
            for tok in range(TOK):
                act.activation(SIG[:, tok, :], SIG[:, tok, :], ACT.Sigmoid).then_inc(sig_done, 1)
            round_unit(UNIT[("br", 0)] + 1)
            round_unit(UNIT[("br", 1)] + 1)
            chain_high("m", 0)
            chain_high("m", 1)
            round_unit(UNIT[("wout", 0)] + 1)
            round_unit(UNIT[("wout", 1)] + 1, (0, 1))
            norm_high("c1", UNIT[("wout", 1)] + 1, True)

            def up_phase(names, nblk, func, chain, late):
                for i, (unit, key) in enumerate(names):
                    u = UNIT[unit]
                    if i == 0 and chain:
                        chain_high(chain, 1)
                    round_unit(u + 1)
                    for tok in range(TOK):
                        act.wait_ge(mm_done, 2 * u + tok + 1)
                        n = P * nblk
                        if TG_READ[key + (tok,)]:
                            act.wait_ge(tmp_v, TG_READ[key + (tok,)])
                        act.activation(TG[:, tok, 0:n], UP[tok][:, 0:n], func).then_inc(tg_done, 1)
                        if tok == 0:
                            for k, dst in late:
                                high(k, dst, n)
                            late = []
                        else:
                            k0 = key_kt(key)
                            high(key + (0,), HH[:, k0:k0 + nblk, 0:P], n)
                            late = [(key + (1,), HH[:, k0:k0 + nblk, P:256])]
                return late

            def down_phase(units, late, n, last=False):
                for i, unit in enumerate(units):
                    at_end = last and i == len(units) - 1
                    round_unit(UNIT[unit] + 1, (0, 1) if at_end else range(4))
                    if i == 0:
                        for k, dst in late:
                            high(k, dst, n)

            for part in range(2):
                g4 = range(4 * part, 4 * part + 4)
                late = up_phase([(("up", g), ("up", g)) for g in g4], 4, ACT.Relu, "c1" if part == 0 else None, [])
                down_phase([("down", g) for g in g4], late, HALF, part == 1)
            norm_high("c2", UNIT[("down", 7)] + 1, True)

            def ffn(f, chain):
                late = up_phase([(("gu", f, c), ("gu", f, c)) for c in range(8)], 2, ACT.Silu, chain, [])
                down_phase([("dn", f, g) for g in range(4)], late, GC)
                late = up_phase([(("gu", f, c), ("gu", f, c)) for c in range(8, 11)], 2, ACT.Silu, None, [])
                down_phase([("dn", f, 4), ("dn", f, 5)], late, GC, True)

            ffn(0, "c2")
            norm_high(("f", 0), UNIT[("dn", 0, 5)] + 1, False)
            att = 2 * NF
            late = None
            for i, c in enumerate((0, 2, 4, 1, 3, 5)):
                u = UNIT[("moba", c)]
                if i == 0:
                    chain_high(("f", 0), 1)
                round_unit(u + 1)
                for tok in range(TOK):
                    act.wait_ge(mm_done, 2 * u + tok + 1)
                    if c < 4:
                        b = TURN[("moba", c, tok)]
                        act.wait_ge(tr_done, b - 1)
                        act.copy(TMP[:, b % 2, :], UP[tok][:, :]).then_inc(tmp_s, 1)
                    else:
                        act.copy(VM[:, tok, (c - 4) * HALF:(c - 3) * HALF], UP[tok][:, :]
                                 ).then_inc(up_copied, 1)
                    if tok == 0 and late:
                        taken(*late)
                        late = None
                    elif tok == 1 and c < 4:
                        dst = (QM if c < 2 else KM)[:, 4 * (c % 2):4 * (c % 2) + 4, :]
                        taken(("moba", c, 0), dst[:, :, 0:P], HALF)
                        late = (("moba", c, 1), dst[:, :, P:256], HALF)
                    if i >= 3 and (tok == 0 or att < 2 * NF + 4):
                        slot(att, 2 * NF, 2 * NF + MH)
                        att += 1
            while att <= 2 * NF + MH:
                slot(att, 2 * NF, 2 * NF + MH)
                att += 1
            for tok in range(TOK):
                chain_high("my", tok)
            round_unit(UNIT[("aout", 0)] + 1)
            round_unit(UNIT[("aout", 1)] + 1, (0, 1))
            norm_high("c3", UNIT[("aout", 1)] + 1, False)
            ffn(1, "c3")
            norm_high(("f", 1), UNIT[("dn", 1, 5)] + 1, False)
            ffn(2, ("f", 1))
            norm_high(("f", 2), UNIT[("dn", 2, 5)] + 1, False)
            chain_high(("f", 2), 1)
            round_unit(UNIT[("bin", 0)] + 1)
            round_unit(UNIT[("bin", 1)] + 1)
            for tok in range(TOK):
                act.wait_ge(mm_done, 2 * UNIT[("bin", 1)] + tok + 1)
                act.copy(UU[:, tok, 0:HALF], Y[tok][0][:, :])
                act.copy(UU[:, tok, HALF:D], Y[tok][1][:, :]).then_inc(uu_done, 1)
            for j in range(4):
                high(("pool", j), HH[:, 2 * j:2 * j + 2, :], HALF)
            round_unit(UNIT[("grp",)] + 1)
            chain_high("g", 0)
            chain_high("g", 1)
            round_unit(UNIT[("bout", 0)] + 1)
            round_unit(UNIT[("bout", 1)] + 1, (0, 1))
            norm_high("c4", UNIT[("bout", 1)] + 1, False)
            ffn(3, "c4")
            for tok in range(TOK):
                squares(("f", 3), tok, False)

        @block.vector
        def _(ve):
            seq = [0]

            def step(ins):
                seq[0] += 1
                ins.then_inc(v_seq, 1)
                ve.wait_ge(v_seq, seq[0])

            def split_unit(u, quarters=range(4)):
                if u >= len(UNITS):
                    return
                _, _, width, kts = UNITS[u]
                n = width * kts // 4
                for q in quarters:
                    ve.wait_ge(wh_done, 4 * u + q + 1)
                    o = slice(q * n, (q + 1) * n)
                    ve.tensor_tensor(WL[:, u % 2, o], RAW[:, q // 2, (q % 2) * n:(q % 2 + 1) * n],
                                     WH[:, u % 2, o].bitcast(F32), ALU.subtract).then_inc(wl_done, 1)

            def low(key, dst, hi, n):
                ve.wait_ge(th_done, SPLIT_NO[key])
                ve.tensor_tensor(dst, TB[TURN[key] % 2][:, 0:n].rearrange("p (k n) -> p k n", n=dst.shape[2]),
                                 hi.bitcast(F32), ALU.subtract).then_inc(tr_free[TURN[key] % 2], 1)

            def chain_low(name, tok, halves=(0, 1)):
                for h in halves:
                    s = (slice(None), slice(4 * h, 4 * h + 4), slice(tok * P, (tok + 1) * P))
                    low((name, tok, h), AL[s], AH[s], HALF)

            def first_low(name, u):
                chain_low(name, 0, (0,))
                split_unit(u, (1,))
                chain_low(name, 0, (1,))
                split_unit(u, (2, 3))

            def plain(key, dst, rows, n):
                ve.wait_ge(tr_done, TURN[key] + 1)
                ve.tensor_copy(dst, TB[TURN[key] % 2][0:rows, 0:n]).then_inc(tr_free[TURN[key] % 2], 1)

            def logits(a):
                kind, h = ITEMS[a]
                z = SB[a % 2]
                ve.wait_ge(s_done, a + 1)
                if kind != "f":
                    scale = P ** -0.5 if kind == "m" else DH ** -0.5
                    z = PR[:, a % 2, :]
                    if a >= 2:
                        ve.wait_ge(pt_tr, a - 1)
                    ve.scalar_tensor_tensor(z[:, 0:P], SB[a % 2][:, 0:P], scale, TAB[:, h, P:TABW],
                                            ALU.mult, ALU.add)
                    step(ve.scalar_tensor_tensor(z[:, P:REV], SB[a % 2][:, P:REV], scale, TAB[:, h, :],
                                                 ALU.mult, ALU.add))
                elif a >= 2:
                    ve.wait_ge(p_done, a - 1)
                ve.tensor_reduce(NM[:, a % 2, 0:1], z[:, 0:P], AX.X, ALU.max, negate=True)
                ve.tensor_reduce(NM[:, a % 2, 1:2], z[:, P:REV], AX.X, ALU.max, negate=True).then_inc(m_done, 1)

            def slot(a, first, end):
                if a < end:
                    logits(a)
                if first < a <= end:
                    ve.wait_ge(p_done, a)
                    ve.reciprocal(RC[:, (a - 1) % 2, :], SM[:, (a - 1) % 2, :]).then_inc(rc_done, 1)

            def stats(tok):
                for h in range(2):
                    ins = ve.bn_stats(ST[:, tok, 6 * h:6 * h + 6], X[:, tok, h * HALF:(h + 1) * HALF])
                step(ins)
                step(ve.bn_aggr(MV[:, tok, :], ST[:, tok, :]))
                ve.scalar_tensor_tensor(VAR[:, tok:tok + 1], MV[:, tok, 0:1], MV[:, tok, 0:1],
                                        MV[:, tok, 1:2], ALU.mult, ALU.add).then_inc(var_done, 1)

            def centre(tok, rms, gain):
                for h in range(2):
                    s = slice(h * HALF, (h + 1) * HALF)
                    if rms:
                        ins = ve.tensor_tensor(Z[:, tok, s], X[:, tok, s], gain[:, s], ALU.mult)
                    else:
                        ins = ve.scalar_tensor_tensor(X[:, tok, s], Z[:, tok, s], MEAN[:, tok, 0:1], gain[:, s],
                                                      ALU.subtract, ALU.mult)
                step(ins)

            def scaled(name, tok, rms, dst, offset, signal):
                ve.wait_ge(rs_done, 2 * CHAIN[name] + tok + 1)
                src = Z if rms else X
                for h in range(2):
                    s = slice(h * HALF, (h + 1) * HALF)
                    if offset is None:
                        ins = ve.tensor_scalar(dst[:, tok, s], src[:, tok, s], RS[:, tok:tok + 1], None, ALU.mult)
                    else:
                        ins = ve.scalar_tensor_tensor(dst[:, tok, s], src[:, tok, s], RS[:, tok:tok + 1],
                                                      offset[:, s], ALU.mult, ALU.add)
                    ins.then_inc(signal, 1)

            def norms(name, unit, begin, rms, gain, offset, dst, turned=True):
                u = UNIT[unit] + 1
                signal = tmp_v if turned else out_ready
                begin(0)
                split_unit(u, (1,))
                centre(0, rms, gain)
                scaled(name, 0, rms, dst, offset, signal)
                begin(1)
                if turned:
                    chain_low(name, 0)
                split_unit(u, (2,))
                centre(1, rms, gain)
                split_unit(u, (3,))
                scaled(name, 1, rms, dst, offset, signal)

            ve.wait_ge(g_seq, CONSTANTS)
            ve.tensor_copy(CMR[:, :], CM[:, :])
            ve.tensor_copy(IDR[:, :], IDENT[:, :]).then_inc(cmr_done, 1)
            ve.wait_ge(in_c, 16)
            acc = ADA[:, 0:2, :].rearrange("p a n -> p (a n)")
            for k in range(KT):
                ve.wait_ge(in_wada[k % 4], 16 * (k // 4 + 1))
                if k == 0:
                    ins = ve.tensor_scalar(acc, WADA[:, 0, :], CC[:, 0:1], None, ALU.mult)
                else:
                    ins = ve.scalar_tensor_tensor(acc, WADA[:, k % 4, :], CC[:, k:k + 1], acc, ALU.mult, ALU.add)
                ins.then_inc(wada_used, 1)
                ve.wait_ge(wada_used, k + 1)
                if k == 3:
                    ve.wait_ge(in_x, 16)
                    for tok in range(TOK):
                        stats(tok)
                if k == 5:
                    for tok in range(TOK):
                        ve.wait_ge(rs_done, tok + 1)
                        ins = ve.tensor_scalar(Z[:, tok, :], X[:, tok, :], RS[:, tok:tok + 1], None, ALU.mult)
                    step(ins)
                    plain(("tab", 0), REVROW[:, :], 8, REV)
            ve.wait_ge(in_rows, 16)

            def modulated(tok, h):
                s = slice(h * HALF, (h + 1) * HALF)
                if tok == 0:
                    ve.wait_ge(ada_done, 2 * h + 2)
                    step(ve.scalar_tensor_tensor(ADA[:, 1, s], Y[1][h][:, :], 1.0, ROWS[:, 0, s], ALU.add, ALU.mult))
                step(ve.tensor_tensor(Z[:, tok, s], Z[:, tok, s], ADA[:, 1, s], ALU.mult))
                ve.tensor_tensor(Z[:, tok, s], Z[:, tok, s], Y[0][h][:, :], ALU.add).then_inc(tmp_v, 1)

            modulated(0, 0)
            modulated(0, 1)
            chain_low("h", 0)
            split_unit(0)
            modulated(1, 0)
            modulated(1, 1)
            chain_low("h", 1)

            piece = [0]

            def modulation(n):
                for _ in range(n):
                    i = piece[0]
                    if i >= 32:
                        return
                    if i == 0:
                        ve.wait_ge(in_bias, 16)
                    ve.wait_ge(in_piece[i % 2], 16 * (i // 2 + 1))
                    dst = ADA[:, i // KT, :]
                    ve.scalar_tensor_tensor(dst, PIECE[:, i % 2, :], CC[:, i % KT:i % KT + 1], dst,
                                            ALU.mult, ALU.add).then_inc(piece_used, 1)
                    ve.wait_ge(piece_used, i + 1)
                    piece[0] += 1

            def forget_in(tok):
                ve.wait_ge(tmp_s, tok + 1)
                ve.tensor_scalar(WI[:, tok, :], UP[tok][:, 320:324], NI ** -0.5, None, ALU.mult)
                ve.tensor_tensor(LF[:, tok, 0, :], UP[tok][:, 324:332], BF[:, :], ALU.add).then_inc(lf_in, 1)

            def forget_out(tok):
                ve.wait_ge(lf_mid, tok + 1)
                ve.scalar_tensor_tensor(LFS[:, tok, :], LF[:, tok, 0, :], 0.0, LF[:, tok, 2, :],
                                        ALU.min, ALU.subtract).then_inc(lf_done, 1)

            def index_scores():
                ve.wait_ge(rev_out, 16)
                for h in range(NI):
                    ve.wait_ge(r_done, h + 1)
                    for tok, lo, hi in ((0, 0, P), (1, P, REV)):
                        r, w = PR[:, 0, lo:hi], WI[:, tok, h:h + 1]
                        if h == 0:
                            ins = ve.tensor_scalar(PR[:, 1, lo:hi], r, w, 0.0, ALU.mult, ALU.add)
                        else:
                            ins = ve.scalar_tensor_tensor(PR[:, 1, lo:hi], r, w, PR[:, 1, lo:hi],
                                                          ALU.mult, ALU.add)
                    ins.then_inc(r_used, 1)
                    ve.wait_ge(r_used, h + 1)
                ve.tensor_tensor(PR[:, 1, 0:P], PR[:, 1, 0:P], CM[:, P:TABW], ALU.add)
                step(ve.tensor_tensor(PR[:, 1, P:REV], PR[:, 1, P:REV], CM[:, :], ALU.add))

            def top_keys(lo, hi):
                for _ in range(TOPK // 8):
                    step(ve.max(M8[:, :], PR[:, 1, lo:hi]))
                    step(ve.match_replace(PR[:, 1, lo:hi], M8[:, :], PR[:, 1, lo:hi], TAKEN))
                ve.tensor_scalar(SELM[:, lo:hi], PR[:, 1, lo:hi], TAKEN / 3, MASKED, ALU.is_gt, ALU.mult
                                 ).then_inc(sel_done, 1)

            att = 0
            for u in range(11):
                split_unit(u + 1)
                if u == 0:
                    forget_in(0)
                    forget_out(0)
                if u >= 4:
                    slot(att, 0, 2 * NF)
                    att += 1
                if u == 0:
                    forget_in(1)
                    forget_out(1)
                if u == 1:
                    ve.wait_ge(tr_done, TURN[("F",)] + 1)
                    ve.tensor_scalar(FT[:, :], TB[TURN[("F",)] % 2][0:NF, 0:256], 1.0, None, ALU.mult)
                    ve.tensor_scalar(FTN[:, :], TB[TURN[("F",)] % 2][0:NF, 0:256], -1.0, None, ALU.mult
                                     ).then_inc(tr_free[TURN[("F",)] % 2], 1)
                    index_scores()
                if u == 2:
                    top_keys(0, P)
                if u == 3:
                    top_keys(P, REV)
                    ve.wait_ge(in_tab, 16)
                if u >= 4:
                    slot(att, 0, 2 * NF)
                    att += 1
                modulation(MODULATION[u])
            while att <= 2 * NF:
                slot(att, 0, 2 * NF)
                att += 1
            for tok in range(TOK):
                chain_low("y", tok)
            for b in range(2):
                u = UNIT[("br", b)]
                split_unit(u + 1, range(4) if b == 0 else (0,))
                ve.wait_ge(sig_done, TOK)
                for tok in range(TOK):
                    ve.wait_ge(mm_done, 2 * u + tok + 1)
                    for h in range(2):
                        g = SIG[:, tok, (1 - b) * D + h * HALF:(1 - b) * D + (h + 1) * HALF]
                        z = Z[:, tok, h * HALF:(h + 1) * HALF] if b == 0 else g
                        ins = ve.tensor_tensor(z, Y[tok][h][:, :], g, ALU.mult)
                    ins.then_inc(y_free[tok], 1)
                    ve.wait_ge(y_free[tok], b + 1)
                    for h in range(2 if b == 1 else 0):
                        s = slice(h * HALF, (h + 1) * HALF)
                        ve.tensor_tensor(Z[:, tok, s], Z[:, tok, s], SIG[:, tok, s], ALU.add).then_inc(tmp_v, 1)
                    if b == 1 and tok == 0:
                        first_low("m", u + 1)
                    elif b == 1:
                        chain_low("m", 1)
            split_unit(UNIT[("wout", 0)] + 1)
            for c in range(4, 10):
                plain(("ada", c), ADA[:, (c - 4) // 2, (c % 2) * HALF:(c % 2 + 1) * HALF], P, HALF)
            ve.wait_ge(in_rows, 48)
            for c in (8, 9):
                ve.wait_ge(*emptied(TURN[("ada", c)]))
            step(ve.scalar_tensor_tensor(ADA[:, 2, :], ADA[:, 2, :], 1.0, ROWS[:, 0, :], ALU.add, ALU.mult))

            def gated(u, tok, gate):
                ve.wait_ge(mm_done, 2 * u + tok + 1)
                for h in range(2):
                    s = slice(h * HALF, (h + 1) * HALF)
                    ins = ve.tensor_tensor(Z[:, tok, s], Y[tok][h][:, :], gate[:, s], ALU.mult)
                ins.then_inc(y_free[tok], 1)
                ve.wait_ge(y_free[tok], DEEP["wout" if gate is ADA_G1 else "mlp"] + 1)
                ve.tensor_tensor(X[:, tok, :], X[:, tok, :], Z[:, tok, :], ALU.add).then_inc(sums_done, 1)
                ve.wait_ge(sums_done, 2 * CHAIN["c1" if gate is ADA_G1 else "c2"] + tok - 1)

            ADA_G1 = ADA[:, 0, :]
            ADA_G2 = ADA[:, 3, :]
            split_unit(UNIT[("wout", 1)] + 1, (0,))
            norms("c1", ("wout", 1), lambda tok: gated(UNIT[("wout", 1)], tok, ADA_G1), True,
                  ADA[:, 2, :], ADA[:, 1, :], Z)

            def up_phase(names, nblk, square, chain, late):
                for i, (unit, key) in enumerate(names):
                    u = UNIT[unit]
                    if i == 0 and chain:
                        chain_low(chain, 1)
                    split_unit(u + 1)
                    n = P * nblk
                    for tok in range(TOK):
                        b = TURN[key + (tok,)]
                        ve.wait_ge(tg_done, TG_NO[key + (tok,)])
                        ve.wait_ge(tr_done, b - 1)
                        other = TG[:, tok, 0:n] if square else UP[tok][:, n:2 * n]
                        ve.tensor_tensor(TMP[:, b % 2, 0:n], TG[:, tok, 0:n], other, ALU.mult).then_inc(tmp_v, 1)
                        if tok == 0:
                            for k, s in late:
                                low(k, HL[s], HH[s], n)
                            late = []
                        else:
                            k0 = key_kt(key)
                            low(key + (0,), HL[:, k0:k0 + nblk, 0:P], HH[:, k0:k0 + nblk, 0:P], n)
                            late = [(key + (1,), (slice(None), slice(k0, k0 + nblk), slice(P, 256)))]
                return late

            def down_phase(units, late, n, pieces=0, last=False):
                for i, unit in enumerate(units):
                    at_end = last and i == len(units) - 1
                    split_unit(UNIT[unit] + 1, (0,) if at_end else range(4))
                    if i == 0:
                        for k, s in late:
                            low(k, HL[s], HH[s], n)
                    modulation(pieces)

            for part in range(2):
                g4 = range(4 * part, 4 * part + 4)
                late = up_phase([(("up", g), ("up", g)) for g in g4], 4, True, "c1" if part == 0 else None, [])
                down_phase([("down", g) for g in g4], late, HALF, 2 if part == 0 else 0, part == 1)
                if part == 0:
                    for c in (10, 11):
                        plain(("ada", c), ADA_G2[:, (c % 2) * HALF:(c % 2 + 1) * HALF], P, HALF)
            norms("c2", ("down", 7), lambda tok: gated(UNIT[("down", 7)], tok, ADA_G2), True,
                  ROWS[:, 1, :], None, X)

            def layer_norm(name, unit, product, factor, rows, turned=True):
                def begin(tok):
                    ve.wait_ge(mm_done, 2 * UNIT[unit] + tok + 1)
                    for h in range(2):
                        s = slice(h * HALF, (h + 1) * HALF)
                        ins = ve.scalar_tensor_tensor(Z[:, tok, s], Y[tok][h][:, :], factor, X[:, tok, s],
                                                      ALU.mult, ALU.add, accum_out=SUMS[:, tok, h:h + 1])
                    ins.then_inc(y_free[tok], 1)
                    ve.wait_ge(y_free[tok], DEEP[product] + 1)
                    s0, s1 = SUMS[:, tok, 0:1], SUMS[:, tok, 1:2]
                    ve.tensor_scalar(MEAN[:, tok, 1:2], s0, s1, -D ** -1.5, ALU.add, ALU.mult).then_inc(sums_done, 1)
                    step(ve.tensor_scalar(MEAN[:, tok, 0:1], s0, s1, 1 / D, ALU.add, ALU.mult))
                    if tok == 0:
                        ve.wait_ge(in_rows, 48 + 32 * (rows + 1))

                norms(name, unit, begin, False, ROWS[:, 0, :], ROWS[:, 1, :], X, turned)

            def ffn(f, chain):
                late = up_phase([(("gu", f, c), ("gu", f, c)) for c in range(8)], 2, False, chain, [])
                down_phase([("dn", f, g) for g in range(4)], late, GC)
                late = up_phase([(("gu", f, c), ("gu", f, c)) for c in range(8, 11)], 2, False, None, [])
                down_phase([("dn", f, 4), ("dn", f, 5)], late, GC, last=True)

            ffn(0, "c2")
            layer_norm(("f", 0), ("dn", 0, 5), "f0", 0.5 / ALPHA, 0)
            att = 2 * NF
            for i, c in enumerate((0, 2, 4, 1, 3, 5)):
                if i == 0:
                    chain_low(("f", 0), 1)
                    plain(("tab", 1), REVROW[:, :], 8, REV)
                split_unit(UNIT[("moba", c)] + 1)
                for tok in range(TOK):
                    if i >= 3 and (tok == 0 or att < 2 * NF + 4):
                        if att == 2 * NF:
                            ve.wait_ge(in_tab, 32)
                        slot(att, 2 * NF, 2 * NF + MH)
                        att += 1
            while att <= 2 * NF + MH:
                slot(att, 2 * NF, 2 * NF + MH)
                att += 1
            for tok in range(TOK):
                chain_low("my", tok)
            split_unit(UNIT[("aout", 0)] + 1)
            split_unit(UNIT[("aout", 1)] + 1, (0,))
            layer_norm("c3", ("aout", 1), "aout", 1 / ALPHA, 1)
            ffn(1, "c3")
            layer_norm(("f", 1), ("dn", 1, 5), "f1", 0.5 / ALPHA, 2)
            ffn(2, ("f", 1))
            layer_norm(("f", 2), ("dn", 2, 5), "f2", 0.5 / ALPHA, 3)
            chain_low(("f", 2), 1)
            split_unit(UNIT[("bin", 0)] + 1)
            split_unit(UNIT[("bin", 1)] + 1)
            for j in range(4):
                low(("pool", j), HL[:, 2 * j:2 * j + 2, :], HH[:, 2 * j:2 * j + 2, :], HALF)
            split_unit(UNIT[("grp",)] + 1, (0,))
            for tok in range(TOK):
                ve.wait_ge(mm_done, 2 * UNIT[("grp",)] + tok + 1)
                for h in range(2):
                    s = slice(h * HALF, (h + 1) * HALF)
                    ins = ve.tensor_tensor(Z[:, tok, s], Y[tok][h][:, :], ADA[:, 0, s], ALU.mult)
                    ins.then_inc(tmp_v, 1)
                if tok == 0:
                    first_low("g", UNIT[("grp",)] + 1)
                else:
                    chain_low("g", 1)
            split_unit(UNIT[("bout", 0)] + 1)
            split_unit(UNIT[("bout", 1)] + 1, (0,))
            layer_norm("c4", ("bout", 1), "bout", 1 / ALPHA, 4)
            ffn(3, "c4")
            layer_norm(("f", 3), ("dn", 3, 5), "f3", 0.5 / ALPHA, 5, turned=False)


_INS = ["x", "c", "w_ada", "b_ada", "g_norm1", "w_in", "b_forget", "rel_bias", "w_branch_fox", "w_branch_dsa",
        "w_out", "g_norm2", "w_mlp1", "w_mlp2", "g_final", "rel_bias_2", "ln_g_2", "ln_b_2", "ffn_w_gu_2",
        "ffn_w_down_2", "a_w_in_2", "a_w_out_2", "b_w_in_2", "b_w_group_2", "b_scale_2", "b_w_out_2"]


def reversed_buckets():
    x = np.arange(REV)
    dist = 2 * P - 1 - x
    n = np.maximum(dist, 0)
    exact = NB // 2
    big = exact + (np.log(np.maximum(n, 1).astype(np.float32) / np.float32(exact))
                   / np.float32(np.log(128 / exact)) * np.float32(NB - exact)).astype(np.int32)
    bucket = np.where(n < exact, n, np.minimum(big, NB - 1))
    hot = np.zeros((NB + 1, REV), np.float32)
    hot[np.where(dist >= 0, bucket, NB), x] = 1.0
    return hot


def pooling():
    m = np.zeros((P, len(WINDOWS), TOK, TOK * P), np.float32)
    for g, w in enumerate(WINDOWS):
        for tt in range(TOK * P):
            for s in range(max(0, tt - w + 1), tt + 1):
                m[s % P, g, s // P, tt] += np.float32(1.0 / min(tt + 1, w))
            m[tt % P, g, tt // P, tt] -= 1.0
    return m


def kernel(**inputs):
    import concourse.bacc as _bacc
    from concourse.bass_utils import run_bass_kernel_spmd as _run

    nc = _bacc.Bacc("TRN2", target_bir_lowering=False, num_devices=1)
    arrays, tensors = {}, {}
    given = {name: inputs[name] for name in _INS}
    given["onehot"] = reversed_buckets()
    given["pool_m"] = pooling()
    for name, a in given.items():
        a = np.ascontiguousarray(a)
        arrays[f"in_{name}"] = a
        tensors[name] = nc.dram_tensor(f"in_{name}", a.shape, mybir.dt.from_np(a.dtype), kind="ExternalInput").ap()
    out = nc.dram_tensor("out_0", (1, TOK * P, D), F32, kind="ExternalOutput").ap()
    build(nc, tensors, out)
    r = _run(nc, [arrays], core_ids=[0])
    return r.results[0]["out_0"]
```
